# Optimizing a Trainium2 kernel written in Bass

```python
import math
import jax, jax.numpy as jnp
from jax import lax
import numpy as np

D_MODEL = 1024
BATCH = 1
SEQ = 128
DEPTH = 2
DEC_BATCH = 1
DEC_SEQ = 512
PAST_LEN = 128

GRID_W = 64
N_BRANCH = 4
BRANCH_W = 512
POOL_WINDOWS = (2, 4, 8, 16)
POOL_GROUP = BRANCH_W // len(POOL_WINDOWS)
NAT_HEADS = 8
NAT_HD = 64
NAT_WIN_R = 8
NAT_WIN_C = 16
NAT_QBLK = 16
NAT_KBLK = 2 * NAT_WIN_C
CONV_W = 31
DIFF_HEADS = 4
DIFF_HD = 64
POOL_IN = BRANCH_W
NAT_IN = 3 * NAT_HEADS * NAT_HD
CONV_IN = 2 * BRANCH_W
DIFF_IN = 2 * (DIFF_HEADS * 2 * DIFF_HD) + DIFF_HEADS * 2 * DIFF_HD
IN_COLS = POOL_IN + NAT_IN + CONV_IN + DIFF_IN
PEER_HEADS = 8
PEER_NKEYS = 128
PEER_N = PEER_NKEYS * PEER_NKEYS
PEER_DK = 256
PEER_TOPK = 16
PEER_CHUNK = 128
QBLOCK = 128
ROPE_BASE = 10000.0
EPS = 1e-6
NEG_INF = -1e30

kernel_name = 'hybrid_diffusion_pool_nat_conv_diff_peer_step'

F32 = jnp.float32

def rms_norm(x, g):
    xf = x.astype(F32)
    y = xf * lax.rsqrt(jnp.mean(xf * xf, axis=-1, keepdims=True) + EPS)
    return (y * g.astype(F32)).astype(x.dtype)

def layer_norm(x, g, b):
    xf = x.astype(F32)
    mu = jnp.mean(xf, axis=-1, keepdims=True)
    var = jnp.mean(jnp.square(xf - mu), axis=-1, keepdims=True)
    y = (xf - mu) * lax.rsqrt(var + EPS) * g.astype(F32) + b.astype(F32)
    return y.astype(x.dtype)

def modulation(cvec, w_ada, b_ada):
    mod = jax.nn.silu(cvec) @ w_ada + b_ada
    return jnp.split(mod[:, None, :], 6, axis=-1)

def modulate(x, g, shift, scale):
    return rms_norm(x, g) * (1 + scale) + shift

def map_query_blocks(fn, q):
    B, L = q.shape[:2]
    nb = L // QBLOCK
    qb = jnp.moveaxis(q.reshape((B, nb, QBLOCK) + q.shape[2:]), 1, 0)
    out = lax.map(fn, qb)
    return jnp.moveaxis(out, 0, 1).reshape((B, L) + out.shape[3:])

def axial_rope(x):
    L, hd = x.shape[1], x.shape[-1]
    half = hd // 2
    quarter = half // 2
    t = jnp.arange(L)
    freqs = ROPE_BASE ** (-jnp.arange(quarter, dtype=F32) / quarter)

    def rot(xa, pos):
        ang = pos.astype(F32)[:, None] * freqs
        cos = jnp.cos(ang)[None, :, None, :]
        sin = jnp.sin(ang)[None, :, None, :]
        x1 = xa[..., :quarter].astype(F32)
        x2 = xa[..., quarter:].astype(F32)
        return jnp.concatenate([x1 * cos - x2 * sin, x1 * sin + x2 * cos], axis=-1)

    out = jnp.concatenate([rot(x[..., :half], t // GRID_W), rot(x[..., half:], t % GRID_W)], axis=-1)
    return out.astype(x.dtype)

def pool_branch(u, pool_w, pool_scale):
    B, L, C = u.shape
    uf = u.astype(F32)
    cs = jnp.concatenate([jnp.zeros((B, 1, C), F32), jnp.cumsum(uf, axis=1)], axis=1)
    t = jnp.arange(L)
    outs = []
    for gi, w in enumerate(POOL_WINDOWS):
        sl = slice(gi * POOL_GROUP, (gi + 1) * POOL_GROUP)
        lo = jnp.clip(t - w // 2, 0, L)
        hi = jnp.clip(t + (w - w // 2), 0, L)
        csg = cs[..., sl]
        mean = (csg[:, hi] - csg[:, lo]) / (hi - lo).astype(F32)[None, :, None]
        d = (mean - uf[..., sl]).astype(u.dtype)
        outs.append(jnp.einsum('blc,ce->ble', d, pool_w[gi]))
    return jnp.concatenate(outs, axis=-1) * pool_scale

def conv_branch(z, conv_w, conv_b, ln_g, ln_b):
    a, b = jnp.split(z, 2, axis=-1)
    u = a * jax.nn.sigmoid(b)
    y = lax.conv_general_dilated(u, conv_w[:, None, :].astype(u.dtype), window_strides=(1,),
                                 padding=[(CONV_W // 2, CONV_W // 2)],
                                 dimension_numbers=('NWC', 'WIO', 'NWC'),
                                 feature_group_count=BRANCH_W) + conv_b
    return jax.nn.silu(layer_norm(y, ln_g, ln_b))

def softmax_attend(q, k, v):
    scale = q.shape[-1] ** -0.5

    def blk(qb):
        s = jnp.einsum('bqhd,bkhd->bhqk', qb, k, preferred_element_type=F32) * scale
        p = jax.nn.softmax(s, axis=-1).astype(v.dtype)
        return jnp.einsum('bhqk,bkhd->bqhd', p, v)

    return map_query_blocks(blk, q)

def nat_latent(q, k, v, ck, cv, rel_bias):
    B, L, H, hd = q.shape
    rows = L // GRID_W
    kr = min(NAT_WIN_R, rows)
    nj = GRID_W // NAT_QBLK
    scale = hd ** -0.5
    r = jnp.arange(rows)
    row_idx = jnp.clip(r - kr // 2, 0, rows - kr)[:, None] + jnp.arange(kr)[None, :]
    j = jnp.arange(nj)
    col_idx = jnp.clip(j * NAT_QBLK - NAT_WIN_C // 2, 0, GRID_W - NAT_KBLK)[:, None] + jnp.arange(NAT_KBLK)[None, :]

    def gather(a):
        ag = a.reshape(B, rows, GRID_W, H, hd)
        blk = ag[:, row_idx[:, None, :, None], col_idx[None, :, None, :]]
        return blk.reshape(B, rows, nj, kr * NAT_KBLK, H, hd)

    kb = gather(k)
    vb = gather(v)
    qg = q.reshape(B, rows, nj, NAT_QBLK, H, hd)
    s_loc = jnp.einsum('brjqhd,brjkhd->bhrjqk', qg, kb, preferred_element_type=F32) * scale
    qcol = j[:, None] * NAT_QBLK + jnp.arange(NAT_QBLK)[None, :]
    wstart = jnp.clip(qcol - NAT_WIN_C // 2, 0, GRID_W - NAT_WIN_C)
    kcol_rel = col_idx[:, None, :] - wstart[:, :, None]
    valid = (kcol_rel >= 0) & (kcol_rel < NAT_WIN_C)
    dcol = col_idx[:, None, :] - qcol[:, :, None]
    drow = row_idx - r[:, None]
    bias = rel_bias[:, (drow + NAT_WIN_R - 1)[:, None, None, :, None],
                    jnp.clip(dcol + NAT_WIN_C - 1, 0, 2 * NAT_WIN_C - 2)[None, :, :, None, :]]
    nloc = kr * NAT_KBLK
    bias = bias.reshape(H, rows, nj, NAT_QBLK, nloc).astype(F32)
    mask = jnp.broadcast_to(valid[:, :, None, :], (nj, NAT_QBLK, kr, NAT_KBLK)).reshape(nj, NAT_QBLK, nloc)
    s_loc = jnp.where(mask[None, None, None], s_loc + bias[None], NEG_INF)
    s_ctx = jnp.einsum('brjqhd,bchd->bhrjqc', qg, ck, preferred_element_type=F32) * scale
    p = jax.nn.softmax(jnp.concatenate([s_loc, s_ctx], axis=-1), axis=-1).astype(v.dtype)
    out = (jnp.einsum('bhrjqk,brjkhd->brjqhd', p[..., :nloc], vb)
           + jnp.einsum('bhrjqc,bchd->brjqhd', p[..., nloc:], cv))
    return out.reshape(B, L, H * hd)

def diff_split(z):
    B, L, _ = z.shape
    nq = DIFF_HEADS * 2 * DIFF_HD
    q = z[..., :nq].reshape(B, L, DIFF_HEADS, 2, DIFF_HD)
    k = z[..., nq:2 * nq].reshape(B, L, DIFF_HEADS, 2, DIFF_HD)
    v = z[..., 2 * nq:].reshape(B, L, DIFF_HEADS, 2 * DIFF_HD)
    return q, k, v

def diff_lambda(lam_p, l):
    lam_init = 0.8 - 0.6 * math.exp(-0.3 * l)
    lf = lam_p.astype(F32)
    lam = jnp.exp(jnp.sum(lf[0] * lf[1])) - jnp.exp(jnp.sum(lf[2] * lf[3])) + lam_init
    return lam, lam_init

def diff_attend(q, ks, vs, lam):
    scale = q.shape[-1] ** -0.5

    def blk(qb):
        s = jnp.concatenate([jnp.einsum('bqhid,bkhid->bhiqk', qb, kk, preferred_element_type=F32) for kk in ks], axis=-1) * scale
        p = jax.nn.softmax(s, axis=-1)
        pd = (p[:, :, 0] - lam * p[:, :, 1]).astype(vs[0].dtype)
        out = 0
        off = 0
        for vv in vs:
            n = vv.shape[1]
            out = out + jnp.einsum('bhqk,bkhe->bqhe', pd[..., off:off + n], vv)
            off += n
        return out

    return map_query_blocks(blk, q)

def merge_branches(h, branches, w_branch, w_gate, b_gate, w_out):
    gates = jax.nn.sigmoid(h @ w_gate + b_gate)
    merged = 0
    for i, y in enumerate(branches):
        merged = merged + gates[..., i * D_MODEL:(i + 1) * D_MODEL] * (y @ w_branch[i])
    return merged @ w_out

def mixer(h, lp, l, ctx):
    B, L, _ = h.shape
    z = h @ lp['w_in']
    o1 = POOL_IN
    o2 = o1 + NAT_IN
    o3 = o2 + CONV_IN
    zp, zn, zc, zd = z[..., :o1], z[..., o1:o2], z[..., o2:o3], z[..., o3:]
    y_pool = pool_branch(zp, lp['pool_w'], lp['pool_scale'])
    qn, kn, vn = [a.reshape(B, L, NAT_HEADS, NAT_HD) for a in jnp.split(zn, 3, axis=-1)]
    qn = rms_norm(qn, lp['nat_q_g'])
    kn = rms_norm(kn, lp['nat_k_g'])
    y_conv = conv_branch(zc, lp['conv_w'], lp['conv_b'], lp['conv_ln_g'], lp['conv_ln_b'])
    qd, kd, vd = diff_split(zd)
    qd = rms_norm(qd, lp['diff_q_g'])
    kd = rms_norm(kd, lp['diff_k_g'])
    lam, lam_init = diff_lambda(lp['diff_lambda_p'], l)
    if ctx is None:
        y_nat = softmax_attend(qn, kn, vn).reshape(B, L, BRANCH_W)
        o_diff = diff_attend(qd, (kd,), (vd,), lam)
        new_ctx = (kn, vn, kd, vd)
    else:
        ck_n, cv_n, ck_d, cv_d = ctx
        y_nat = nat_latent(qn, kn, vn, ck_n, cv_n, lp['nat_rel_bias'])
        qd = axial_rope(qd.reshape(B, L, 2 * DIFF_HEADS, DIFF_HD)).reshape(qd.shape)
        kd = axial_rope(kd.reshape(B, L, 2 * DIFF_HEADS, DIFF_HD)).reshape(kd.shape)
        o_diff = diff_attend(qd, (kd, ck_d), (vd, cv_d), lam)
        new_ctx = None
    y_diff = (rms_norm(o_diff, lp['diff_subln_g']) * (1 - lam_init)).reshape(B, L, BRANCH_W)
    out = merge_branches(h, (y_pool, y_nat, y_conv, y_diff), lp['w_branch'], lp['w_gate'], lp['b_gate'], lp['w_out'])
    return out, new_ctx

def peer_ffn(h, w_query, sub_keys, u_tab, v_tab):
    B, L, D = h.shape
    nc = (B * L) // PEER_CHUNK

    def chunk(hc):
        qry = (hc @ w_query).reshape(-1, PEER_HEADS, 2, PEER_DK // 2)
        s = jnp.einsum('thpk,hpnk->thpn', qry, sub_keys, preferred_element_type=F32)
        s1, i1 = lax.top_k(s[:, :, 0], PEER_TOPK)
        s2, i2 = lax.top_k(s[:, :, 1], PEER_TOPK)
        cand = (s1[..., :, None] + s2[..., None, :]).reshape(-1, PEER_HEADS, PEER_TOPK * PEER_TOPK)
        sc, ci = lax.top_k(cand, PEER_TOPK)
        e = (jnp.take_along_axis(i1, ci // PEER_TOPK, axis=-1) * PEER_NKEYS
             + jnp.take_along_axis(i2, ci % PEER_TOPK, axis=-1))
        g = jax.nn.softmax(sc, axis=-1)
        act = jax.nn.gelu(jnp.einsum('thkd,td->thk', u_tab[e], hc, preferred_element_type=F32), approximate=False)
        return jnp.einsum('thk,thkd->td', (g * act).astype(hc.dtype), v_tab[e])

    y = lax.map(chunk, h.reshape(nc, PEER_CHUNK, D))
    return y.reshape(B, L, D)

def trunk_layer(x, mod, lp, l, ctx):
    sh1, sc1, g1, sh2, sc2, g2 = mod
    h = modulate(x, lp['norm1_g'], sh1, sc1)
    y, new_ctx = mixer(h, lp, l, ctx)
    x = x + g1 * y
    h = modulate(x, lp['norm2_g'], sh2, sc2)
    x = x + g2 * peer_ffn(h, lp['peer_w_query'], lp['peer_sub_keys'], lp['peer_u'], lp['peer_v'])
    return x, new_ctx

def setup_inputs(seed: int = 0) -> dict:
    key = jax.random.key(seed)
    ks = iter(jax.random.split(key, 48))
    D = D_MODEL

    def nrm(shape, s):
        return jax.random.normal(next(ks), shape, F32) * s

    def gain(shape):
        return 1.0 + nrm(shape, 0.02)

    return {
        'x_prompt': nrm((BATCH, SEQ, D), 1.0),
        'x_sample': nrm((DEC_BATCH, DEC_SEQ, D), 1.0),
        'cache_nat_k': nrm((DEC_BATCH, DEPTH, PAST_LEN, NAT_HEADS, NAT_HD), 1.0),
        'cache_nat_v': nrm((DEC_BATCH, DEPTH, PAST_LEN, NAT_HEADS, NAT_HD), 1.0),
        'cache_diff_k': nrm((DEC_BATCH, DEPTH, PAST_LEN, DIFF_HEADS, 2, DIFF_HD), 1.0),
        'cache_diff_v': nrm((DEC_BATCH, DEPTH, PAST_LEN, DIFF_HEADS, 2 * DIFF_HD), 1.0),
        'c': nrm((DEC_BATCH, D), 1.0),
        'c_ctx': nrm((D,), 1.0),
        'w_ada': nrm((DEPTH, D, 6 * D), 0.5 * D ** -0.5),
        'b_ada': nrm((DEPTH, 6 * D), 0.02),
        'norm1_g': gain((DEPTH, D)),
        'norm2_g': gain((DEPTH, D)),
        'w_in': nrm((DEPTH, D, IN_COLS), D ** -0.5),
        'pool_w': nrm((DEPTH, len(POOL_WINDOWS), POOL_GROUP, POOL_GROUP), POOL_GROUP ** -0.5),
        'pool_scale': gain((DEPTH, BRANCH_W)),
        'nat_q_g': gain((DEPTH, NAT_HD)),
        'nat_k_g': gain((DEPTH, NAT_HD)),
        'nat_rel_bias': nrm((DEPTH, NAT_HEADS, 2 * NAT_WIN_R - 1, 2 * NAT_WIN_C - 1), 0.1),
        'conv_w': nrm((DEPTH, CONV_W, BRANCH_W), CONV_W ** -0.5),
        'conv_b': nrm((DEPTH, BRANCH_W), 0.02),
        'conv_ln_g': gain((DEPTH, BRANCH_W)),
        'conv_ln_b': nrm((DEPTH, BRANCH_W), 0.02),
        'diff_q_g': gain((DEPTH, DIFF_HD)),
        'diff_k_g': gain((DEPTH, DIFF_HD)),
        'diff_lambda_p': nrm((DEPTH, 4, DIFF_HD), 0.1),
        'diff_subln_g': gain((DEPTH, 2 * DIFF_HD)),
        'w_branch': nrm((DEPTH, N_BRANCH, BRANCH_W, D), BRANCH_W ** -0.5),
        'w_gate': nrm((DEPTH, D, N_BRANCH * D), D ** -0.5),
        'b_gate': nrm((DEPTH, N_BRANCH * D), 0.02),
        'w_out': nrm((DEPTH, D, D), D ** -0.5),
        'peer_w_query': nrm((DEPTH, D, PEER_HEADS * PEER_DK), D ** -0.5),
        'peer_sub_keys': nrm((DEPTH, PEER_HEADS, 2, PEER_NKEYS, PEER_DK // 2), (PEER_DK // 2) ** -0.5),
        'peer_u': nrm((DEPTH, PEER_N, D), D ** -0.5),
        'peer_v': nrm((DEPTH, PEER_N, D), PEER_HEADS ** -0.5),
    }

def reference(x_prompt, x_sample, cache_nat_k, cache_nat_v, cache_diff_k, cache_diff_v, c, c_ctx,
              w_ada, b_ada, norm1_g, norm2_g, w_in, pool_w, pool_scale, nat_q_g, nat_k_g, nat_rel_bias,
              conv_w, conv_b, conv_ln_g, conv_ln_b, diff_q_g, diff_k_g, diff_lambda_p, diff_subln_g,
              w_branch, w_gate, b_gate, w_out, peer_w_query, peer_sub_keys, peer_u, peer_v):
    xp = x_prompt
    xs = x_sample
    nat_ks, nat_vs, diff_ks, diff_vs = [], [], [], []
    for l in range(DEPTH):
        lp = {
            'norm1_g': norm1_g[l], 'norm2_g': norm2_g[l], 'w_in': w_in[l],
            'pool_w': pool_w[l], 'pool_scale': pool_scale[l],
            'nat_q_g': nat_q_g[l], 'nat_k_g': nat_k_g[l], 'nat_rel_bias': nat_rel_bias[l],
            'conv_w': conv_w[l], 'conv_b': conv_b[l], 'conv_ln_g': conv_ln_g[l], 'conv_ln_b': conv_ln_b[l],
            'diff_q_g': diff_q_g[l], 'diff_k_g': diff_k_g[l], 'diff_lambda_p': diff_lambda_p[l],
            'diff_subln_g': diff_subln_g[l],
            'w_branch': w_branch[l], 'w_gate': w_gate[l], 'b_gate': b_gate[l], 'w_out': w_out[l],
            'peer_w_query': peer_w_query[l], 'peer_sub_keys': peer_sub_keys[l],
            'peer_u': peer_u[l], 'peer_v': peer_v[l],
        }
        mod_ctx = modulation(c_ctx[None, :], w_ada[l], b_ada[l])
        xp, (nk, nv, dk, dv) = trunk_layer(xp, mod_ctx, lp, l, None)
        nat_ks.append(nk)
        nat_vs.append(nv)
        diff_ks.append(dk)
        diff_vs.append(dv)
        mod_lat = modulation(c, w_ada[l], b_ada[l])
        ctx = (cache_nat_k[:, l], cache_nat_v[:, l], cache_diff_k[:, l], cache_diff_v[:, l])
        xs, _ = trunk_layer(xs, mod_lat, lp, l, ctx)
    state_nat_k = jnp.stack(nat_ks, axis=1)
    state_nat_v = jnp.stack(nat_vs, axis=1)
    state_diff_k = jnp.stack(diff_ks, axis=1)
    state_diff_v = jnp.stack(diff_vs, axis=1)
    return (xp, xs, state_nat_k, state_nat_v, state_diff_k, state_diff_v)


_drawn_inputs = setup_inputs


def setup_inputs(seed=0):
    import zlib

    import numpy as np

    out = dict(_drawn_inputs(seed))
    spreads = {}
    factors = {'cache_nat_k': 3.671,
     'cache_nat_v': 3.012,
     'norm1_g': 2.883,
     'norm2_g': 18.779,
     'pool_scale': 8.0,
     'nat_q_g': 22.898,
     'nat_k_g': 2.741,
     'nat_rel_bias': 46.443,
     'conv_b': 7.957,
     'conv_ln_g': 56.345,
     'conv_ln_b': 52.844,
     'diff_q_g': 8.0,
     'diff_lambda_p': 4.626,
     'diff_subln_g': 50.433,
     'b_gate': 8.0}
    for name, (base, spread) in spreads.items():
        noise = np.random.default_rng([zlib.crc32(name.encode()), seed]).standard_normal(out[name].shape)
        drawn = base * np.exp(spread * noise) if base else spread * noise
        out[name] = __import__('jax').numpy.asarray(drawn.astype(out[name].dtype))
    for name, factor in factors.items():
        out[name] = (out[name] * factor).astype(out[name].dtype)
    return out
```

```python
from contextlib import ExitStack

import concourse.bass as bass
import numpy as np
from concourse import mybir

F32 = mybir.dt.float32
U32 = mybir.dt.uint32
ALU = mybir.AluOpType
ACT = mybir.ActivationFunctionType
AX_X = mybir.AxisListType.X
ds = bass.ds

P = 128
D = 1024
KD = D // P
SEQ, LAT, PAST = 128, 512, 128
TOK = LAT + SEQ
NT = TOK // P
NL = LAT // P
HT = P // 2
DEPTH = 2
EPS = 1e-6
NEG_INF = -1e30
GRID_W, ROWS = 64, 8
NJ, QB, KB = 4, 16, 32
WIN_C, WIN_R = 16, 8
COL0 = [min(max(j * QB - WIN_C // 2, 0), GRID_W - KB) for j in range(NJ)]
CONV_W = 31
POOL_WINDOWS = (2, 4, 8, 16)
PAD = 16
LAT0, CTX0 = PAD, 2 * PAD + LAT
PADDED = 3 * PAD + TOK
SPAN = CTX0 + SEQ - LAT0
BW = 512
HEADS, NKEYS, TOPK = 8, 128, 16
NEXP = NKEYS * NKEYS
LOWEST = -3.0e38

RING = 6
C_ADA, C_CONV, C_POOL, C_V, C_QK, C_MERGE, C_OUT, C_QUERY, NCHUNK = 0, 48, 56, 60, 68, 84, 132, 140, 156
USES = NCHUNK // RING

S_BADA, S_N1, S_N2, S_PSC, S_CW, S_CB, S_LG, S_LB, S_SUB, S_BG = 0, 48, 56, 64, 68, 192, 196, 200, 204, 205
NSMALL = 237

UNITS = ["rms1"] + [f"ada{n}" for n in range(12)] + ["mod"]
for _c in range(4):
    UNITS += [f"cb{_c}", f"ca{_c}"]
UNITS += [f"pl{g}" for g in range(4)]
UNITS += [f"dv{t}" for t in range(NT)] + [f"nv{t}" for t in range(NT)]
QK = [(b, t) for b in ("dq", "dk", "nq", "nk") for t in range(NT)]
UNITS += [f"{b}{t}" for b, t in QK]
UNITS += ["lnm", "lnv"] + [f"pw{g}" for g in range(4)] + [f"dr{h}" for h in range(4)]
UNITS += [f"o{d}" for d in range(KD)] + ["rms2", "q0"]
for _n in range(1, 16):
    UNITS += [f"q{_n}", f"s{_n - 1}"]
UNITS += ["s15"] + [f"hn{t}" for t in range(NT)] + [f"yn{t}" for t in range(NT)]
UNIT = {u: n for n, u in enumerate(UNITS)}
TURNS = len(UNITS) // 3
assert TURNS * 3 == len(UNITS)
FIN0 = DEPTH * len(UNITS)

READY = ["rms1", "mod"] + [f"dv{t}" for t in range(NT - 1)] + [f"nv{t}" for t in range(NT - 1)]
READY += [f"{b}{t}" for b, t in QK if t < NT - 1]
READY += ["lnm", "lnv"] + [f"pw{g}" for g in range(4)] + [f"dr{h}" for h in range(4)] + ["rms2"]
READY += [f"s{n}" for n in range(16)] + [f"hn{t}" for t in range(NT)] + [f"yn{t}" for t in range(NT)]
READY_AT = {u: n for n, u in enumerate(READY)}
CHUNK_OF = {f"cb{c}": C_CONV + 2 * i for i, c in enumerate(range(4))}
CHUNK_OF |= {f"ca{c}": C_CONV + 2 * i + 1 for i, c in enumerate(range(4))}
CHUNK_OF |= {f"pl{g}": C_POOL + g for g in range(4)}
CHUNK_OF |= {f"dv{NT - 1}": C_V + 3, f"nv{NT - 1}": C_V + 7}
CHUNK_OF |= {f"{b}{NT - 1}": C_QK + 4 * i + 3 for i, b in enumerate(("dq", "dk", "nq", "nk"))}
CHUNK_OF |= {f"o{d}": C_OUT + d for d in range(KD)} | {f"q{n}": C_QUERY + n for n in range(16)}

JOBS = [("diff", h, t) for h in range(4) for t in range(NT)]
JOBS += [("nat", h, j) for h in range(8) for j in range(NT)]
NJOBS = len(JOBS)
MAPS = [2 if kind == "diff" else 1 for kind, _, _ in JOBS]
MAP0 = [sum(MAPS[:n]) for n in range(NJOBS)]
NMAPS = sum(MAPS)

GRP = 4
SLOTS = 2 * GRP
GRPS = TOPK // GRP
BODIES = NT * HEADS // 2
CHAIN_LAYER = 4096
CHAIN_BODY = 128
CHAIN_TILE = 4 * CHAIN_BODY + 8


class Chain:

    def __init__(self, eng, sem):
        self.eng, self.sem, self.base, self.n = eng, sem, 0, 0

    def tick(self, ins, to=None):
        step = 1 if to is None else to - self.n
        assert step > 0
        ins.then_inc(self.sem, step)
        self.n += step

    def wait(self):
        self.eng.wait_ge(self.sem, self.base + self.n)

    def link(self, ins, to=None):
        self.tick(ins, to)
        self.wait()


def backbone(nc, xT, cT, w, small, rowg, lamrow, clay, poolw, subk, rope, edge, mask, bias, ckn, ckd,
             cvn, cvd, experts, y_prompt, y_sample, o_nk, o_nv, o_dk, o_dv):
    with ExitStack() as cx:
        def sb(name, shape, dt=F32):
            return cx.enter_context(nc.sbuf_tensor(name, shape, dt))

        def sem(name):
            return cx.enter_context(nc.semaphore(name))

        vscr = nc.dram_tensor("v_scratch", (LAT, BW), F32, kind="Internal").ap()

        x_sb = sb("x_sb", [P, NT, KD, P])
        h_sb = sb("h_sb", [P, NT, KD, P])
        wring = sb("wring", [P, RING, 1024])
        arena = sb("arena", [P, 29696])
        bsb = sb("bsb", [P, 2064])
        T = sb("T", [P, 3200])
        sm = sb("sm", [P, NSMALL])
        rg = sb("rg", [P, 256])
        cl = sb("cl", [P, 4])
        mod = sb("mod_sb", [P, 48, 2])
        amp = sb("amp", [P, 2, KD, 2])
        ident = sb("ident", [P, P])
        ones = sb("ones", [P, P])
        rp = sb("rp", [P, NL, 2, 64])
        ed = sb("ed", [P, 4, 16])
        mk = sb("mk", [P, NJ, KB])
        csil = sb("csil", [P, KD, 2])
        lam = sb("lam", [P, 8])
        st = sb("st", [P, 48])
        ps = cx.enter_context(nc.psum_tensor("ps", [P, 8, 512], F32))

        def at(tensor, start, *shape):
            n = int(np.prod(shape))
            v = tensor[:, start:start + n]
            if len(shape) == 1:
                return v
            names = "abcd"[:len(shape)]
            return v.rearrange(f"p ({' '.join(names)}) -> p {' '.join(names)}", **dict(zip(names, shape)))

        yT = at(arena, 0, 16, TOK)
        acc = at(arena, 4 * TOK, 4, SPAN)
        U = at(arena, 4 * TOK + 4 * SPAN, 4, PADDED)
        vst = at(arena, 16 * TOK - 1024, 2, BW)
        pw_sb = at(arena, 16 * TOK - 1536, 4, P)
        A0, B0 = 16 * TOK, 16 * TOK + 8704
        dqT, dkT, dv = at(arena, A0, 4, TOK), at(arena, A0 + 2560, 4, 768), at(arena, A0 + 5632, 6, BW)
        nqT, nkT = at(arena, B0, 4, TOK), at(arena, B0 + 2560, 4, 768)
        vwin, nv = at(arena, B0 + 5632, 8, BW), at(arena, B0 + 5632 + 4096, 2, BW)
        modrow = arena[0:2, B0:B0 + 6 * D]
        sq = at(arena, A0, NT, KD, P)
        xs = at(arena, 0, NT, KD, P)
        merged = at(arena, A0, KD, TOK)
        gt = at(arena, B0, 2, TOK)
        prod = at(arena, B0 + 2 * TOK, 2, TOK)
        rstd = at(T, 0, TOK)
        scores = at(arena, 0, NT * 16 + 2, NKEYS)
        SC_END = (NT * 16 + 2) * NKEYS
        rows = at(arena, SC_END, SLOTS, 2 * D)
        sk = at(arena, SC_END + SLOTS * 2 * D, 16, NKEYS)
        qst = at(T, 0, 2, TOK)
        sc = at(T, 0, 2, NKEYS)
        screp = at(T, 256, 2, NKEYS)
        cand = at(T, 512, TOPK, TOPK)
        crep = at(T, 768, 256)
        hot = at(T, 1024, 2, TOPK, TOPK)
        top = at(T, 1536, 2, TOPK)
        topf = at(T, 1568, 2, TOPK)
        csc = at(T, 1600, 2, TOPK)
        abf = at(T, 1632, 2, TOPK)
        sel = at(T, 1664, 2, TOPK)
        ef = at(T, 1696, TOPK)
        gate = at(T, 1712, 2, TOPK)
        dots = at(T, 1744, 2, TOPK)
        gel = at(T, 1776, 2, TOPK)
        wgt = at(T, 1808, 2, TOPK)
        iota = at(T, 1840, TOPK)
        topi = sb("topi", [P, 2, TOPK], U32)
        ci = sb("ci", [P, 3, TOPK], U32)
        eidx = sb("eidx", [P, 2, TOPK], U32)
        iota_i = sb("iota_i", [P, TOPK], mybir.dt.int32)
        dg = at(bsb, 0, 2, GRP, P)

        w_load = [sem(f"w_load{i}") for i in range(RING)]
        w_done = [sem(f"w_done{i}") for i in range(RING)]
        free = [sem(f"pair_free{i}") for i in range(3)]
        ready = sem("unit_ready")
        const_in, ctab = sem("const_in"), sem("ctab")
        params, lam_in, pool_in, ctx_in, subk_in = [sem(n) for n in ("params", "lam_in", "pool_in", "ctx_in", "subk_in")]
        csil_ok, lam_exp = sem("csil_ok"), sem("lam_exp")
        lam_sum = sem("lam_sum")
        x_ready, sq_ready, root, h_ready = sem("x_ready"), sem("sq_ready"), sem("root"), sem("h_ready")
        u_ready, conv_pool, conv_done, pool_d = sem("u_ready"), sem("conv_pool"), sem("conv_done"), sem("pool_d")
        vb_out, vb_in, state_out = [sem(f"vb_out{i}") for i in range(2)], sem("vb_in"), sem("state_out")
        qk_sq, qk_ms, qk_root, qk_fin, qk_evac, qk_tr = [sem(n) for n in ("qk_sq", "qk_ms", "qk_root", "qk_fin", "qk_evac", "qk_tr")]
        cen_ok, csq, cms, croot, cnorm, y_conv = [sem(n) for n in ("cen_ok", "csq", "cms", "croot", "cnorm", "y_conv")]
        bias_in, bias_ok = [sem(f"bias_in{i}") for i in range(2)], sem("bias_ok")
        s_ready, m_ready, exp_done, pd_ready, t_ready, pt_evac, o_ready, o_evac = [
            sem(n) for n in ("s_ready", "m_ready", "exp_done", "pd_ready", "t_ready", "pt_evac", "o_ready", "o_evac")]
        dsq, droot, y_diff = sem("dsq"), sem("droot"), sem("y_diff")
        br_ready, gate_evac, br_evac, merged_ok = sem("br_ready"), sem("gate_evac"), sem("br_evac"), sem("merged_ok")
        gath = [sem(f"gath{i}") for i in range(SLOTS)]
        idx_ready, top_ready, gexp, dot, gelu_ok, dg_ready, v_done, y_zero = [
            sem(n) for n in ("idx_ready", "top_ready", "gexp", "dot", "gelu_ok", "dg_ready", "v_done", "y_zero")]
        dve_own, act_own, pool_own = sem("dve_own"), sem("act_own"), sem("pool_own")
        out_done = sem("out_done")

        def pair(u, it=0):
            return UNIT[u] % 3

        def wait_free(eng, l, u, more=0):
            eng.wait_ge(free[pair(u)], l * TURNS + (UNIT[u] // 3 + 1) + more)

        def wait_unit(eng, l, u):
            if u in READY_AT:
                eng.wait_ge(ready, l * len(READY) + (READY_AT[u] + 1))
            else:
                eng.wait_ge(w_done[CHUNK_OF[u] % RING], l * USES + (CHUNK_OF[u] // RING + 1))

        def wait_chunk(eng, l, c, turn=0):
            eng.wait_ge(w_load[c % RING], (l * USES + (c // RING + 1) + turn) * 16)

        def wait_count(eng, s, l, per_layer, n):
            eng.wait_ge(s, l * per_layer + n)

        def pause(eng):
            eng.nop(nofuse=True)

        def banks(u):
            b = 2 * pair(u)
            return ps[:, b, :], ps[:, b + 1, 0:P]

        def halves(u):
            b = 2 * pair(u)
            return halves_at(b)

        def halves_at(b):
            return ps[:, b:b + 2, 0:TOK // 2].rearrange("p s (t c) -> p t s c", c=HT)

        def by_half(ap):
            return ap.rearrange("p (t s c) -> p t s c", s=2, c=HT)

        def split_half(ap3):
            return ap3.rearrange("p t (s c) -> p t s c", c=HT)

        def both(u):
            b = 2 * pair(u)
            return ps[:, b:b + 2, :].rearrange("p b c -> p (b c)")

        def tile4(ap):
            return ap.rearrange("p (t c) -> p t c", c=P)

        def job_width(kind, t):
            return SEQ if t == NL else (TOK if kind == "diff" else ROWS * KB + PAST)

        def map_banks(m):
            b = 2 * (m % 2)
            return ps[:, b:b + 2, :].rearrange("p b c -> p (b c)")

        def job_out(act, l, n, own, wait_count):
            kind, h, t = JOBS[n]
            wait_count(act, o_ready, l, NJOBS, n + 1)
            src = ps[:, 6 + n % 2, 0:P]
            if kind == "diff":
                op = act.activation(yT[:, 12 + h, t * P:(t + 1) * P], src, ACT.Copy)
            else:
                lo = 64 * (h % 2)
                row = yT[lo:lo + 64, 8 + h // 2, :]
                if t == NL:
                    op = act.activation(row[:, LAT:TOK], src[lo:lo + 64, :], ACT.Copy)
                else:
                    dst = row[:, 0:LAT].rearrange("p (r c) -> p r c", c=GRID_W)[:, :, t * QB:(t + 1) * QB]
                    op = act.activation(dst, src[lo:lo + 64, :].rearrange("p (r c) -> p r c", c=QB), ACT.Copy)
            op.then_inc(o_evac, 1)

        block = cx.enter_context(nc.Block())

        @block.sync
        def _(sp):
            for s in range(RING):
                sp.dma_start(wring[:, s, :], w[s]).then_inc(w_load[s], 16)
            with sp.Fori(1, DEPTH * USES) as turn:
                for s in range(RING):
                    sp.wait_ge(w_done[s], turn)
                    pause(sp)
                    sp.dma_start(wring[:, s, :], w[ds(turn * RING + s, 1)].rearrange("a p n -> (a p) n")).then_inc(w_load[s], 16)
            sp.wait_ge(out_done, 16 * NT)
            sp.wait_ge(state_out, 16 * 4 * DEPTH)

        @block.gpsimd
        def _(gp):
            own = Chain(gp, pool_own)
            gp.dma_start(x_sb[:], xT).then_inc(const_in, 16)
            gp.dma_start(csil[:], cT).then_inc(ctab, 16)
            gp.dma_start(rp[:], rope).then_inc(const_in, 16)
            gp.dma_start(ed[:], edge).then_inc(const_in, 16)
            gp.dma_start(mk[:], mask).then_inc(const_in, 16)
            own.link(gp.memset(ident[:], 0.0))
            own.link(gp.affine_select(out=ident[:], in_=ident[:], compare_op=ALU.not_equal, fill=1.0, base=0,
                                      pattern=[[-1, P]], channel_multiplier=1))
            own.link(gp.memset(ones[:], 1.0))
            gp.wait_ge(const_in, 64)
            own.tick(gp.iota(iota_i[:], pattern=[[1, TOPK]], base=0, channel_multiplier=0), to=8)

            with gp.Fori(0, DEPTH) as l:
                own.base, own.n = l * CHAIN_LAYER + 8, 0
                wait_count(gp, x_ready, l, 2, 1)
                pause(gp)
                gp.dma_start(sm[:], small[ds(l, 1)].rearrange("a p n -> (a p) n")).then_inc(params, 16)
                gp.dma_start(rg[:], rowg[ds(l * P, P)]).then_inc(params, 16)
                gp.dma_start(cl[:], clay[ds(l, 1)].rearrange("a p n -> (a p) n")).then_inc(params, 16)
                gp.dma_start(at(T, 640, 256), lamrow[ds(l * P, P)]).then_inc(lam_in, 16)
                wait_count(gp, h_ready, l, 2, 1)
                wait_count(gp, lam_sum, l, 1, 1)
                pause(gp)
                own.tick(gp.memset(U, 0.0))
                own.link(gp.memset(at(bsb, 0, 3, PADDED), 0.0))
                gp.dma_start(pw_sb, poolw[ds(l, 1)].rearrange("a p g c -> (a p) g c")).then_inc(pool_in, 16)
                gp.dma_start(dkT[:, :, TOK:TOK + PAST], ckd[ds(l, 1)].rearrange("a p h c -> (a p) h c")).then_inc(ctx_in, 16)
                gp.dma_start(nkT[:, :, TOK:TOK + PAST], ckn[ds(l, 1)].rearrange("a p h c -> (a p) h c")).then_inc(ctx_in, 16)
                gp.dma_start(dv[:, 5, :], cvd[ds(l, 1)].rearrange("a p c -> (a p) c")).then_inc(ctx_in, 16)
                gp.dma_start(nv[:, 1, :], cvn[ds(l, 1)].rearrange("a p c -> (a p) c")).then_inc(ctx_in, 16)
                gp.sem_inc(conv_pool, 1)

                u, sA, sB = (at(bsb, i * PADDED, PADDED) for i in range(3))
                for g, win in enumerate(POOL_WINDOWS):
                    wait_free(gp, l, f"pl{g}", 1)
                    pause(gp)
                    own.tick(gp.tensor_copy(u[:, LAT0:LAT0 + LAT], yT[:, g, 0:LAT]))
                    own.link(gp.tensor_copy(u[:, CTX0:CTX0 + SEQ], yT[:, g, LAT:TOK]))
                    src, dst, half = u, sA, 1
                    lo, hi = 1, PADDED
                    pause(gp)
                    own.link(gp.tensor_tensor(dst[:, lo:hi], src[:, lo - 1:hi - 1], src[:, lo:hi], ALU.add))
                    while 2 * half < win:
                        src, dst = dst, (sB if dst is sA else sA)
                        lo, hi = lo + half, hi - half
                        pause(gp)
                        own.link(gp.tensor_tensor(dst[:, lo:hi], src[:, lo - half:hi - half], src[:, lo + half:hi + half], ALU.add))
                        half *= 2
                    other = sB if dst is sA else sA
                    pause(gp)
                    own.link(gp.tensor_scalar(other[:, LAT0:LAT0 + SPAN], dst[:, LAT0:LAT0 + SPAN], 1.0 / win, None, ALU.mult))
                    for s in (LAT0, LAT0 + LAT - 8, CTX0, CTX0 + SEQ - 8):
                        e = 0 if s in (LAT0, CTX0) else 8
                        pause(gp)
                        own.tick(gp.tensor_tensor(other[:, s:s + 8], dst[:, s:s + 8], ed[:, g, e:e + 8], ALU.mult))
                    own.wait()
                    pause(gp)
                    own.tick(gp.tensor_tensor(yT[:, g, 0:LAT], other[:, LAT0:LAT0 + LAT], u[:, LAT0:LAT0 + LAT], ALU.subtract))
                    gp.tensor_tensor(yT[:, g, LAT:TOK], other[:, CTX0:CTX0 + SEQ], u[:, CTX0:CTX0 + SEQ], ALU.subtract).then_inc(pool_d, 1)
                    wait_count(gp, pool_d, l, 4, g + 1)

                for i in range(2):
                    wait_count(gp, vb_out[i], l * 16, 2, 32)
                pause(gp)
                vg = vscr.rearrange("(r c) n -> r c n", c=GRID_W)
                for j in range(NJ):
                    for half in range(2):
                        for r in range(4):
                            gp.dma_start(vwin[32 * r:32 * r + 32, 2 * j + half, :],
                                         vg[4 * half + r, COL0[j]:COL0[j] + KB, :]).then_inc(vb_in, 16)

                wait_count(gp, pool_d, l, 4, 4)
                for h in range(8):
                    if h >= 2:
                        wait_count(gp, m_ready, l, NMAPS, MAP0[20 + NT * (h - 2) + NJ])
                    pause(gp)
                    bh = at(bsb, (h % 2) * 1024, NJ, ROWS * KB)
                    gp.dma_start(bh, bias[ds(l * 8 + h, 1)].rearrange("a p j k -> (a p) j k")).then_inc(bias_in[h % 2], 16)
                    gp.wait_ge(bias_in[h % 2], (l * 4 + (h // 2 + 1)) * 16)
                    pause(gp)
                    for j in range(NJ):
                        b3 = bh[:, j, :].rearrange("p (r k) -> p r k", k=KB)
                        op = gp.tensor_tensor(b3, b3, mk[:, j:j + 1, :].broadcast_to([P, ROWS, KB]), ALU.add)
                        op.then_inc(bias_ok, 1)

                wait_count(gp, h_ready, l, 2, 2)
                pause(gp)
                gp.dma_start(sk, subk[ds(l, 1)].rearrange("a p h c -> (a p) h c")).then_inc(subk_in, 16)
                pause(gp)
                with gp.Fori(0, BODIES) as b:
                    for hh in range(2):
                        gp.wait_ge(idx_ready, l * (HEADS * NT + 1) + b * 2 + (hh + 1))
                        for e in range(TOPK):
                            s = e % SLOTS
                            gp.wait_ge(v_done, l * (BODIES * 2 * TOPK) + b * (2 * TOPK) + (hh * TOPK + e + 1))
                            pause(gp)
                            gp.indirect_dma_start(rows[:, s, :], None, experts,
                                                  bass.IndirectOffsetOnAxis(ap=eidx[:, hh, e:e + 1], axis=0)).then_inc(gath[s], 16)
                pause(gp)
                own.tick(gp.memset(st[:, 47:48], 0.0), to=CHAIN_LAYER)

        @block.scalar
        def _(act):
            own = Chain(act, act_own)
            act.wait_ge(ctab, 16)
            act.activation(csil[:], csil[:], ACT.Silu).then_inc(csil_ok, 1)

            with act.Fori(0, DEPTH) as l:
                own.base, own.n = l * CHAIN_LAYER, 0

                def squares(which):
                    wait_count(act, x_ready, l, 2, which)
                    if which == 2:
                        wait_unit(act, l, f"o{KD - 1}")
                    for t in range(NT):
                        act.activation(sq[:, t], x_sb[:, t], ACT.Square).then_inc(sq_ready, 1)
                    wait_free(act, l, f"rms{which}", 1)
                    act.activation(rstd, rstd, ACT.Sqrt).then_inc(root, 1)

                squares(1)
                pause(act)
                with act.Fori(0, 4) as it:
                    for b in range(3):
                        c = 4 * b + 3
                        pr = (b + 1) % 3
                        act.wait_ge(w_done[c % RING], l * USES + it * 2 + (c // RING + 1))
                        pause(act)
                        act.activation(modrow[:, ds(it * 1536 + b * 512, 512)], ps[0:2, 2 * pr, :], ACT.Copy).then_inc(free[pr], 1)
                wait_count(act, lam_sum, l, 1, 1)
                act.activation(lam[:, 2:4], lam[:, 0:2], ACT.Exp).then_inc(lam_exp, 1)

                for i, c in enumerate(range(4)):
                    wait_unit(act, l, f"cb{c}")
                    if i >= 2:
                        wait_count(act, u_ready, l, 4, i - 1)
                    sg = at(T, 640 + 640 * (i % 2), TOK)
                    if i == 0:
                        wait_count(act, h_ready, l, 2, 1)
                    act.activation(by_half(sg), halves(f"cb{c}"), ACT.Sigmoid).then_inc(free[pair(f"cb{c}")], 1)
                for g in range(4):
                    wait_unit(act, l, f"pl{g}")
                    act.activation(by_half(yT[:, g, :]), halves(f"pl{g}"), ACT.Copy).then_inc(free[pair(f"pl{g}")], 1)
                for t in range(NT):
                    wait_unit(act, l, f"dv{t}")
                    act.activation(dv[:, t, :], banks(f"dv{t}")[0], ACT.Copy).then_inc(free[pair(f"dv{t}")], 1)
                wait_free(act, l, f"dv{NL}", 1)
                pause(act)
                act.dma_start(o_dv[ds(l * P, P)], dv[:, NL, :]).then_inc(state_out, 16)
                for t in range(NL):
                    wait_unit(act, l, f"nv{t}")
                    if t >= 2:
                        wait_count(act, vb_out[t % 2], l * 16, 2, 16)
                    act.activation(vst[:, t % 2, :], banks(f"nv{t}")[0], ACT.Copy).then_inc(free[pair(f"nv{t}")], 1)
                    wait_free(act, l, f"nv{t}", 1)
                    act.dma_start(vscr[t * P:(t + 1) * P, :], vst[:, t % 2, :]).then_inc(vb_out[t % 2], 16)
                wait_unit(act, l, f"nv{NL}")
                act.activation(nv[:, 0, :], banks(f"nv{NL}")[0], ACT.Copy).then_inc(free[pair(f"nv{NL}")], 1)
                wait_free(act, l, f"nv{NL}", 1)
                pause(act)
                act.dma_start(o_nv[ds(l * P, P)], nv[:, 0, :]).then_inc(state_out, 16)

                def qk_square(n):
                    b, t = QK[n]
                    wait_unit(act, l, f"{b}{t}")
                    if n >= 2:
                        wait_count(act, qk_ms, l, 20, n - 1)
                    if n == 0:
                        wait_count(act, u_ready, l, 4, 4)
                    act.activation(at(T, (n % 2) * 512, 512), banks(f"{b}{t}")[0], ACT.Square).then_inc(qk_sq, 1)

                def qk_rt(n):
                    wait_count(act, qk_ms, l, 20, n + 1)
                    act.activation(st[:, (n % 2) * 8:(n % 2) * 8 + 8], st[:, (n % 2) * 8:(n % 2) * 8 + 8], ACT.Sqrt).then_inc(qk_root, 1)

                def qk_out(n):
                    b, t = QK[n]
                    wait_count(act, qk_tr, l, 20, n + 1)
                    src = ps[:, 6 + n % 2, :].rearrange("p (h c) -> p h c", c=P)
                    dst = {"dq": dqT, "dk": dkT, "nq": nqT, "nk": nkT}[b]
                    if b == "nq" and t < NL:
                        for r in range(2):
                            s4 = src[:, :, r * 64:(r + 1) * 64].rearrange("p h (j c) -> p h j c", c=QB)
                            d4 = dst[:, :, 0:LAT].rearrange("p h (j c) -> p h j c", c=P)[:, :, :, (2 * t + r) * QB:(2 * t + r + 1) * QB]
                            op = act.activation(d4, s4, ACT.Copy)
                            if r == 0:
                                own.tick(op)
                    else:
                        op = act.activation(dst[:, :, t * P:(t + 1) * P], src, ACT.Copy)
                    op.then_inc(qk_evac, 1)
                    if b in ("dk", "nk") and t == NL:
                        pause(act)
                        act.dma_start((o_dk if b == "dk" else o_nk)[ds(l * P, P)], at(T, 1024 + (n % 2) * 512, 512)).then_inc(state_out, 16)

                for n in range(len(QK) + 2):
                    if n < len(QK):
                        qk_square(n)
                    if 1 <= n <= len(QK):
                        qk_rt(n - 1)
                    if n >= 2:
                        qk_out(n - 2)

                wait_count(act, cen_ok, l, 1, 1)
                wait_count(act, state_out, l * 16, 4, 64)
                csqv = at(T, 0, 4, TOK)
                for c in range(4):
                    own.tick(act.activation(csqv[:, c, 0:LAT], acc[:, c, 0:LAT], ACT.Square))
                    act.activation(csqv[:, c, LAT:TOK], acc[:, c, SPAN - SEQ:SPAN], ACT.Square).then_inc(csq, 1)
                wait_free(act, l, "lnv", 1)
                act.activation(at(T, 2560, TOK), at(T, 2560, TOK), ACT.Sqrt).then_inc(croot, 1)
                for g in range(4):
                    wait_unit(act, l, f"pw{g}")
                    scl = sm[:, S_PSC + g:S_PSC + g + 1]
                    act.activation(by_half(yT[:, g, :]), halves(f"pw{g}"), ACT.Copy, scale=scl).then_inc(free[pair(f"pw{g}")], 1)
                wait_count(act, cnorm, l, 1, 1)
                for c in range(4):
                    kw = dict(scale=sm[:, S_LG + c:S_LG + c + 1], bias=sm[:, S_LB + c:S_LB + c + 1])
                    own.link(act.activation(yT[:, 4 + c, 0:LAT], acc[:, c, 0:LAT], ACT.Silu, **kw))
                    op = act.activation(yT[:, 4 + c, LAT:TOK], acc[:, c, SPAN - SEQ:SPAN], ACT.Silu, **kw)
                    if c < 3:
                        own.link(op)
                    else:
                        op.then_inc(y_conv, 1)

                def job_exp(n):
                    kind, h, t = JOBS[n]
                    width = job_width(kind, t)
                    o = (n % 2) * 8
                    for i in range(MAPS[n]):
                        m = MAP0[n] + i
                        wait_count(act, m_ready, l, NMAPS, m + 1)
                        act.activation(at(T, (n % 2) * 1280 + i * TOK, width), map_banks(m)[:, 0:width], ACT.Exp,
                                       bias=st[:, o + i:o + i + 1], accum_out=st[:, o + 2 + i:o + 3 + i]).then_inc(exp_done, 1)

                job_exp(0)
                for n, (kind, h, t) in enumerate(JOBS):
                    if n + 1 < NJOBS:
                        job_exp(n + 1)
                    width = job_width(kind, t)
                    wait_count(act, t_ready, l, NJOBS, n + 1)
                    src = ps[:, 4:6, :].rearrange("p b c -> p (b c)")[:, 0:width]
                    act.activation(at(T, 2560, TOK)[:, 0:width], src, ACT.Copy).then_inc(pt_evac, 1)
                    if n:
                        job_out(act, l, n - 1, own, wait_count)
                job_out(act, l, NJOBS - 1, own, wait_count)

                for h in range(4):
                    if h == 0:
                        wait_count(act, o_ready, l, NJOBS, NJOBS)
                        wait_count(act, o_evac, l, NJOBS, NJOBS)
                    if h >= 2:
                        wait_unit(act, l, f"dr{h - 2}")
                    act.activation(at(T, (h % 2) * TOK, TOK), yT[:, 12 + h, :], ACT.Square).then_inc(dsq, 1)
                    if h >= 1:
                        wait_free(act, l, f"dr{h - 1}", 1)
                        r = at(T, 1280 + ((h - 1) % 2) * TOK, TOK)
                        act.activation(r, r, ACT.Sqrt).then_inc(droot, 1)
                wait_free(act, l, "dr3", 1)
                r = at(T, 1280 + TOK, TOK)
                act.activation(r, r, ACT.Sqrt).then_inc(droot, 1)

                pause(act)
                with act.Fori(0, 4) as dp:
                    for n in range(8):
                        i, dd = n // 2, n % 2
                        c = C_MERGE + 3 * i + dd
                        act.wait_ge(w_done[c % RING], l * USES + dp * 2 + (c // RING + 1))
                        act.wait_ge(br_evac, l * 32 + dp * 8 + (n + 1))
                        pause(act)
                        col = sm[:, ds(dp * 2 + (S_BG + 8 * i + dd), 1)]
                        act.activation(by_half(gt[:, n % 2, :]), halves_at(2 * (n % 2)), ACT.Sigmoid, bias=col).then_inc(gate_evac, 1)

                squares(2)

                for n in range(16):
                    if n == 0:
                        wait_count(act, h_ready, l, 2, 2)
                    wait_unit(act, l, f"q{n}")
                    if n >= 2:
                        wait_unit(act, l, f"s{n - 2}")
                    act.activation(by_half(qst[:, n % 2, :]), halves(f"q{n}"), ACT.Copy).then_inc(free[pair(f"q{n}")], 1)
                for t in range(NT):
                    wait_unit(act, l, f"hn{t}")
                    act.activation(h_sb[:, t].rearrange("p k c -> p (k c)"), both(f"hn{t}"), ACT.Copy).then_inc(free[pair(f"hn{t}")], 1)

                def numerators(j, par):
                    act.wait_ge(top_ready, j + 1)
                    act.activation(gate[:, par, :], csc[:, par, :], ACT.Exp, bias=st[:, 16 + par:17 + par],
                                   accum_out=st[:, 18 + par:19 + par]).then_inc(gexp, 1)

                numerators(l * (HEADS * NT + 1), 0)
                pause(act)
                with act.Fori(0, BODIES) as b:
                    for hh in range(2):
                        for g in range(GRPS):
                            if g == 2:
                                numerators(l * (HEADS * NT + 1) + b * 2 + (hh + 1), (hh + 1) % 2)
                            act.wait_ge(dot, l * (BODIES * 2 * TOPK) + b * (2 * TOPK) + (hh * TOPK + (g + 1) * GRP))
                            act.activation(gel[:, hh, g * GRP:(g + 1) * GRP], dots[:, hh, g * GRP:(g + 1) * GRP], ACT.Gelu).then_inc(gelu_ok, 1)
                own.tick(act.activation(st[:, 46:47], ident[:, 0:1], ACT.Copy), to=CHAIN_LAYER)

            for t in range(NT):
                act.wait_ge(ready, DEPTH * len(READY) + t + 1)
                b = 2 * (t % 3)
                o = at(arena, t * D, D)
                act.activation(o, ps[:, b:b + 2, :].rearrange("p b c -> p (b c)"), ACT.Copy).then_inc(free[t % 3], 1)
                act.wait_ge(free[t % 3], DEPTH * TURNS + t // 3 + 2)
                act.dma_start(y_sample[t * P:(t + 1) * P, :] if t < NL else y_prompt, o).then_inc(out_done, 16)

        @block.vector
        def _(v):
            own = Chain(v, dve_own)
            for f in free:
                v.sem_inc(f, 1)
            v.sem_inc(br_evac, 2)
            v.sem_inc(v_done, SLOTS)
            v.wait_ge(const_in, 64)
            v.wait_ge(pool_own, 8)
            v.sem_inc(x_ready, 1)

            with v.Fori(0, DEPTH) as l:
                own.base, own.n = l * CHAIN_LAYER, 0
                S = lambda a, n=1: sm[:, a:a + n]

                def normalise(which):
                    u = f"rms{which}"
                    wait_unit(v, l, u)
                    v.tensor_scalar(by_half(rstd), halves(u), 1.0 / D, EPS, ALU.mult, ALU.add).then_inc(free[pair(u)], 1)
                    wait_count(v, root, l, 2, which)
                    own.link(v.reciprocal(rstd, rstd))
                    for t in range(NT):
                        own.tick(v.tensor_tensor(xs[:, t], x_sb[:, t], rstd[:, t * P:(t + 1) * P].unsqueeze(1).broadcast_to([P, KD, P]), ALU.mult))
                    own.wait()

                def modulate(which):
                    sh = 0 if which == 1 else 24
                    for k in range(KD):
                        own.tick(v.tensor_scalar(h_sb[:, 0:NL, k, :], xs[:, 0:NL, k, :], amp[:, which - 1, k, 0:1], mod[:, sh + k, 0:1], ALU.mult, ALU.add))
                        op = v.tensor_scalar(h_sb[:, NL, k, :], xs[:, NL, k, :], amp[:, which - 1, k, 1:2], mod[:, sh + k, 1:2], ALU.mult, ALU.add)
                        if k < KD - 1:
                            own.tick(op)
                        else:
                            op.then_inc(h_ready, 1)

                normalise(1)

                wait_count(v, params, l * 16, 3, 48)
                wait_count(v, lam_in, l * 16, 1, 16)
                lr = at(T, 640, 2, 2, 64)
                own.link(v.tensor_tensor(at(T, 896, 2, 64), lr[:, :, 0, :], lr[:, :, 1, :], ALU.mult))
                own.link(v.tensor_reduce(lam[:, 0:2], at(T, 896, 2, 64), AX_X, ALU.add))
                v.sem_inc(lam_sum, 1)
                own.tick(v.tensor_scalar(rg[:, 0:64], rg[:, 0:64], 0.125, None, ALU.mult))
                own.tick(v.tensor_scalar(rg[:, 128:192], rg[:, 128:192], 0.125, None, ALU.mult))
                own.link(v.tensor_tensor(lam[:, 5:6], S(S_SUB), cl[:, 1:2], ALU.mult))
                wait_count(v, lam_exp, l, 1, 1)
                own.link(v.tensor_tensor(lam[:, 4:5], lam[:, 3:4], lam[:, 2:3], ALU.subtract))
                own.tick(v.tensor_tensor(lam[:, 4:5], lam[:, 4:5], cl[:, 0:1], ALU.subtract))

                wait_unit(v, l, "mod")
                src = ps[:, 2 * pair("mod"), 0:96].rearrange("p (c s) -> p c s", s=2)
                v.tensor_tensor(mod[:], src, S(S_BADA, 48).unsqueeze(2).broadcast_to([P, 48, 2]), ALU.add).then_inc(free[pair("mod")], 1)
                wait_free(v, l, "mod", 1)
                for i, (sc_at, g_at) in enumerate(((8, S_N1), (32, S_N2))):
                    own.link(v.scalar_tensor_tensor(amp[:, i], mod[:, sc_at:sc_at + 8, :], 1.0,
                                                    S(g_at, 8).unsqueeze(2).broadcast_to([P, 8, 2]), ALU.add, ALU.mult))

                modulate(1)

                wait_count(v, conv_pool, l, 1, 1)
                for i, c in enumerate(range(4)):
                    wait_unit(v, l, f"ca{c}")
                    wait_free(v, l, f"cb{c}", 1)
                    a5 = halves(f"ca{c}")
                    g5 = by_half(at(T, 640 + 640 * (i % 2), TOK))
                    own.tick(v.tensor_tensor(by_half(U[:, c, LAT0:LAT0 + LAT]), a5[:, 0:NL], g5[:, 0:NL], ALU.mult))
                    v.tensor_tensor(by_half(U[:, c, CTX0:CTX0 + SEQ]), a5[:, NL:NT], g5[:, NL:NT], ALU.mult).then_inc(free[pair(f"ca{c}")], 1)
                    wait_free(v, l, f"ca{c}", 1)
                    own.wait()
                    v.sem_inc(u_ready, 1)
                for k in range(CONV_W):
                    for c in range(4):
                        if k:
                            v.wait_ge(dve_own, own.base + own.n - 3)
                            col = S_CW + c * CONV_W + k
                            op = v.scalar_tensor_tensor(acc[:, c, :], U[:, c, 1 + k:1 + k + SPAN], S(col), acc[:, c, :], ALU.mult, ALU.add)
                        else:
                            op = v.tensor_scalar(acc[:, c, :], U[:, c, 1:1 + SPAN], S(S_CW + c * CONV_W), S(S_CB + c), ALU.mult, ALU.add)
                        own.tick(op)
                own.wait()
                v.sem_inc(conv_done, 1)

                def qk_mean(n):
                    b, t = QK[n]
                    o = (n % 2) * 8
                    wait_count(v, qk_sq, l, 20, n + 1)
                    own.link(v.tensor_reduce(st[:, o:o + 8], at(T, (n % 2) * 512, 8, 64), AX_X, ALU.add))
                    v.tensor_scalar(st[:, o:o + 8], st[:, o:o + 8], 1.0 / 64, EPS, ALU.mult, ALU.add).then_inc(qk_ms, 1)

                def qk_norm(n):
                    b, t = QK[n]
                    o = (n % 2) * 8
                    qn = at(T, 1024 + (n % 2) * 512, 8, 64)
                    wait_count(v, qk_root, l, 20, n + 1)
                    own.link(v.reciprocal(st[:, 16 + o:24 + o], st[:, o:o + 8]))
                    if n >= 2:
                        wait_count(v, qk_tr, l, 20, n - 1)
                    if n == 11:
                        wait_count(v, state_out, l * 16, 4, 48)
                    unit = f"{b}{t}"
                    src = banks(unit)[0].rearrange("p (h c) -> p h c", c=64)
                    v.tensor_tensor(qn, src, st[:, 16 + o:24 + o].unsqueeze(2).broadcast_to([P, 8, 64]), ALU.mult).then_inc(free[pair(unit)], 1)
                    wait_free(v, l, unit, 1)
                    g0 = {"nq": 0, "nk": 64, "dq": 128, "dk": 192}[b]
                    gain = rg[:, g0:g0 + 64].unsqueeze(1).broadcast_to([P, 8, 64])
                    if b[0] == "n" or t == NL:
                        v.tensor_tensor(qn, qn, gain, ALU.mult).then_inc(qk_fin, 1)
                        return
                    own.link(v.tensor_tensor(qn, qn, gain, ALU.mult))
                    rot = at(T, 2048, 8, 64)
                    q5 = qn.rearrange("p h (a s f) -> p h a s f", a=2, s=2)
                    r5 = rot.rearrange("p h (a s f) -> p h a s f", a=2, s=2)
                    s4 = rp[:, t, 1, :].rearrange("p (a s f) -> p a s f", a=2, s=2)
                    for s in range(2):
                        for a in range(2):
                            own.tick(v.tensor_tensor(r5[:, :, a, s, :], q5[:, :, a, 1 - s, :], s4[:, a, s, :].unsqueeze(1).broadcast_to([P, 8, 16]), ALU.mult))
                    own.wait()
                    own.link(v.tensor_tensor(qn, qn, rp[:, t, 0, :].unsqueeze(1).broadcast_to([P, 8, 64]), ALU.mult))
                    v.tensor_tensor(qn, qn, rot, ALU.add).then_inc(qk_fin, 1)

                for n in range(len(QK) + 1):
                    if n < len(QK):
                        qk_mean(n)
                    if n >= 1:
                        qk_norm(n - 1)

                def seqs(ap3):
                    return ((ap3[:, :, 0:LAT], 0, LAT), (ap3[:, :, SPAN - SEQ:SPAN], LAT, TOK))

                wait_unit(v, l, "lnm")
                for (a3, s, e), b in zip(seqs(acc), banks("lnm")):
                    n = e - s
                    op = v.scalar_tensor_tensor(a3, b.unsqueeze(1).broadcast_to([P, 4, n]), -1.0 / BW, a3, ALU.mult, ALU.add)
                    if s == 0:
                        own.link(op)
                op.then_inc(free[pair("lnm")], 1)
                wait_free(v, l, "lnm", 1)
                v.sem_inc(cen_ok, 1)
                wait_unit(v, l, "lnv")
                rs = at(T, 2560, TOK)
                b0, b1 = banks("lnv")
                own.tick(v.tensor_scalar(rs[:, 0:LAT], b0, 1.0 / BW, EPS, ALU.mult, ALU.add))
                v.tensor_scalar(rs[:, LAT:TOK], b1, 1.0 / BW, EPS, ALU.mult, ALU.add).then_inc(free[pair("lnv")], 1)
                wait_count(v, croot, l, 1, 1)
                own.link(v.reciprocal(rs, rs))
                for a3, s, e in seqs(acc):
                    op = v.tensor_tensor(a3, a3, rs[:, s:e].unsqueeze(1).broadcast_to([P, 4, e - s]), ALU.mult)
                    if s == 0:
                        own.tick(op)
                op.then_inc(cnorm, 1)

                def job_max(n):
                    kind, h, t = JOBS[n]
                    width = job_width(kind, t)
                    o = (n % 2) * 8
                    for i in range(MAPS[n]):
                        m = MAP0[n] + i
                        wait_count(v, s_ready, l, NMAPS, m + 1)
                        src = map_banks(m)[:, 0:width]
                        if kind == "nat" and t < NL:
                            wait_count(v, bias_ok, l, 32, NJ * h + t + 1)
                            loc = src[:, 0:ROWS * KB]
                            own.link(v.tensor_tensor(loc, loc, at(bsb, (h % 2) * 1024, NJ, ROWS * KB)[:, t, :], ALU.add))
                        own.link(v.tensor_reduce(st[:, o + 4 + i:o + 5 + i], src, AX_X, ALU.max))
                        v.tensor_scalar(st[:, o + i:o + i + 1], st[:, o + 4 + i:o + 5 + i], -1.0, None, ALU.mult).then_inc(m_ready, 1)

                def job_probs(n):
                    kind, h, t = JOBS[n]
                    width = job_width(kind, t)
                    o, maps = (n % 2) * 8, MAPS[n]
                    wait_count(v, exp_done, l, NMAPS, MAP0[n] + maps)
                    P0 = at(T, (n % 2) * 1280, width)
                    P1 = at(T, (n % 2) * 1280 + TOK, width)
                    own.link(v.reciprocal(st[:, o + 6:o + 6 + maps], st[:, o + 2:o + 2 + maps]))
                    op = v.tensor_scalar(P0, P0, st[:, o + 6:o + 7], None, ALU.mult)
                    if kind == "diff":
                        own.tick(op)
                        own.link(v.tensor_tensor(st[:, o + 7:o + 8], st[:, o + 7:o + 8], lam[:, 4:5], ALU.mult))
                        op = v.scalar_tensor_tensor(P0, P1, st[:, o + 7:o + 8], P0, ALU.mult, ALU.add)
                    op.then_inc(pd_ready, 1)

                job_max(0)
                for n in range(NJOBS):
                    if n + 1 < NJOBS:
                        job_max(n + 1)
                    job_probs(n)

                for h in range(4):
                    wait_unit(v, l, f"dr{h}")
                    r = at(T, 1280 + (h % 2) * TOK, TOK)
                    v.tensor_scalar(by_half(r), halves(f"dr{h}"), 1.0 / P, EPS, ALU.mult, ALU.add).then_inc(free[pair(f"dr{h}")], 1)
                    wait_count(v, droot, l, 4, h + 1)
                    own.link(v.reciprocal(r, r))
                    v.scalar_tensor_tensor(yT[:, 12 + h, :], yT[:, 12 + h, :], lam[:, 5:6], r, ALU.mult, ALU.mult).then_inc(y_diff, 1)

                MERGE = 48
                m0, outer = own.n, own.base
                pause(v)
                with v.Fori(0, 4) as dp:
                    own.base, own.n = outer + m0 + dp * MERGE, 0
                    for n in range(8):
                        i, dd = n // 2, n % 2
                        v.wait_ge(gate_evac, l * 32 + dp * 8 + (n + 1))
                        if dd:
                            c = C_MERGE + 3 * i + 2
                            v.wait_ge(w_done[c % RING], l * USES + dp * 2 + (c // RING + 1))
                        else:
                            v.wait_ge(br_ready, l * 16 + dp * 4 + (i + 1))
                        m = merged[:, ds(dp * 2 + dd, 1), :].rearrange("p a c -> p (a c)")
                        dst = m if i == 0 else prod[:, n % 2, :]
                        v.tensor_tensor(by_half(dst), halves_at(4 + 2 * (n % 2)), by_half(gt[:, n % 2, :]), ALU.mult).then_inc(br_evac, 1)
                        if i:
                            v.wait_ge(br_evac, l * 32 + dp * 8 + (n + 3))
                            if i > 1:
                                own.wait()
                            op = v.tensor_tensor(m, m, prod[:, n % 2, :], ALU.add)
                            own.tick(op, to=MERGE if n == 7 else None)
                    own.wait()
                    v.sem_inc(merged_ok, 1)
                own.base, own.n = outer, m0 + 4 * MERGE

                for d in range(KD):
                    u = f"o{d}"
                    wait_unit(v, l, u)
                    o5, x5 = halves(u), split_half(x_sb[:, :, d, :])
                    for s in range(2):
                        own.tick(v.scalar_tensor_tensor(x5[:, 0:NL, s], o5[:, 0:NL, s], mod[:, 16 + d, 0:1], x5[:, 0:NL, s], ALU.mult, ALU.add))
                    v.scalar_tensor_tensor(x5[:, NL:NT], o5[:, NL:NT], mod[:, 16 + d, 1:2], x5[:, NL:NT], ALU.mult, ALU.add).then_inc(free[pair(u)], 1)
                wait_free(v, l, f"o{KD - 1}", 1)
                own.wait()
                v.sem_inc(x_ready, 1)
                normalise(2)
                modulate(2)

                sc4 = scores[:, 0:NT * 16, :].rearrange("p (t n) c -> p t n c", t=NT)
                wait_count(v, h_ready, l, 2, 2)
                own.tick(v.memset(scores[:, NT * 16:NT * 16 + 2, :], 0.0))
                own.tick(v.memset(ps[:, 6:8, :], 0.0))
                for n in range(16):
                    u = f"s{n}"
                    wait_unit(v, l, u)
                    b0, b1 = banks(u)
                    own.tick(v.tensor_copy(sc4[:, 0:NL, n, :], tile4(b0)))
                    v.tensor_copy(sc4[:, NL, n, :], b1).then_inc(free[pair(u)], 1)
                wait_free(v, l, "s15", 1)
                wait_free(v, l, "s14", 1)
                own.tick(v.tensor_copy(iota, iota_i[:]))
                own.wait()
                v.sem_inc(y_zero, 1)

                def route(j, par):
                    own.link(v.tensor_copy(sc, scores[:, ds(j * 2, 2), :]))
                    for p in range(2):
                        pause(v)
                        own.tick(v.max(top[:, p, 0:8], sc[:, p, :]))
                    own.wait()
                    for p in range(2):
                        pause(v)
                        own.tick(v.max_index(topi[:, p, 0:8], top[:, p, 0:8], sc[:, p, :]))
                        pause(v)
                        own.tick(v.match_replace(screp[:, p, :], top[:, p, 0:8], sc[:, p, :], LOWEST))
                    own.wait()
                    for p in range(2):
                        pause(v)
                        own.tick(v.max(top[:, p, 8:16], screp[:, p, :]))
                    own.wait()
                    for p in range(2):
                        pause(v)
                        own.tick(v.max_index(topi[:, p, 8:16], top[:, p, 8:16], screp[:, p, :]))
                    yield
                    own.tick(v.tensor_tensor(cand, top[:, 0, :].unsqueeze(2).broadcast_to([P, TOPK, TOPK]),
                                             top[:, 1, :].unsqueeze(1).broadcast_to([P, TOPK, TOPK]), ALU.add))
                    own.wait()
                    own.tick(v.tensor_copy(topf, topi[:]))
                    flat = cand.rearrange("p a b -> p (a b)")
                    pause(v)
                    own.link(v.max(csc[:, par, 0:8], flat))
                    pause(v)
                    own.tick(v.max_index(ci[:, 0, 0:8], csc[:, par, 0:8], flat))
                    pause(v)
                    own.link(v.match_replace(crep, csc[:, par, 0:8], flat, LOWEST))
                    pause(v)
                    own.link(v.max(csc[:, par, 8:16], crep))
                    v.tensor_scalar(st[:, 16 + par:17 + par], csc[:, par, 0:1], -1.0, None, ALU.mult).then_inc(top_ready, 1)
                    pause(v)
                    own.link(v.max_index(ci[:, 0, 8:16], csc[:, par, 8:16], crep))
                    yield
                    own.tick(v.tensor_scalar(ci[:, 1, :], ci[:, 0, :], 4, None, ALU.logical_shift_right))
                    own.link(v.tensor_scalar(ci[:, 2, :], ci[:, 0, :], 15, None, ALU.bitwise_and))
                    own.link(v.tensor_copy(abf, ci[:, 1:3, :]))
                    for p in range(2):
                        own.tick(v.tensor_tensor(hot[:, p], abf[:, p, :].unsqueeze(2).broadcast_to([P, TOPK, TOPK]),
                                                 iota.unsqueeze(1).broadcast_to([P, TOPK, TOPK]), ALU.is_equal))
                    own.wait()
                    for p in range(2):
                        own.tick(v.tensor_tensor(hot[:, p], hot[:, p], topf[:, p, :].unsqueeze(1).broadcast_to([P, TOPK, TOPK]), ALU.mult))
                    own.wait()
                    own.link(v.tensor_reduce(sel, hot, AX_X, ALU.add))
                    own.link(v.scalar_tensor_tensor(ef, sel[:, 0, :], float(NKEYS), sel[:, 1, :], ALU.mult, ALU.add))
                    v.tensor_scalar(eidx[:, par, :], ef, cl[:, 2:3], None, ALU.add).then_inc(idx_ready, 1)

                def process(hj, gj, hh, steps):
                    for g in range(GRPS):
                        for e in range(GRP):
                            x = g * GRP + e
                            s = x % SLOTS
                            v.wait_ge(gath[s], (gj * 2 + (x // SLOTS + 1)) * 16)
                            pause(v)
                            v.tensor_tensor_reduce(rows[:, s, 0:D], rows[:, s, 0:D], hcur, 1.0, 0.0,
                                                   ALU.mult, ALU.add, dots[:, hh, x:x + 1]).then_inc(dot, 1)
                        if g == 0:
                            v.wait_ge(gexp, hj + 1)
                            own.link(v.reciprocal(st[:, 20 + hh:21 + hh], st[:, 18 + hh:19 + hh]))
                            own.link(v.tensor_scalar(gate[:, hh, :], gate[:, hh, :], st[:, 20 + hh:21 + hh], None, ALU.mult))
                        next(steps, None)
                        v.wait_ge(gelu_ok, gj * GRPS + (g + 1))
                        cols = slice(g * GRP, (g + 1) * GRP)
                        own.link(v.tensor_tensor(wgt[:, hh, cols], gel[:, hh, cols], gate[:, hh, cols], ALU.mult))
                        v.tensor_tensor(dg[:, g % 2], ident[:].unsqueeze(1).broadcast_to([P, GRP, P]),
                                        wgt[:, hh, cols].unsqueeze(2).broadcast_to([P, GRP, P]), ALU.mult).then_inc(dg_ready, 1)

                for _ in route(0, 0):
                    pass
                hcur = at(bsb, 1024, D)
                p0, outer = own.n, own.base
                pause(v)
                with v.Fori(0, NT) as t:
                    own.base, own.n = outer + p0 + t * CHAIN_TILE, 0
                    wait_free(v, l, f"hn{NT - 1}", 1)
                    wait_free(v, l, f"hn{NT - 2}", 1)
                    wait_free(v, l, f"hn{NT - 3}", 1)
                    pause(v)
                    own.link(v.tensor_copy(hcur, h_sb[:, ds(t, 1)].rearrange("p a k c -> p (a k c)")))
                    pause(v)
                    with v.Fori(0, HEADS // 2) as q:
                        own.base, own.n = outer + (p0 + 1) + t * CHAIN_TILE + q * CHAIN_BODY, 0
                        for hh in range(2):
                            steps = route(t * HEADS + q * 2 + (hh + 1), (hh + 1) % 2)
                            before = l * (HEADS * NT) + t * HEADS + q * 2 + hh
                            process(l * (HEADS * NT + 1) + t * HEADS + q * 2 + hh, before, hh, steps)
                        own.link(v.tensor_copy(st[:, 22:23], st[:, 16:17]), to=CHAIN_BODY)
                    own.base, own.n = outer + (p0 + 1) + t * CHAIN_TILE, 4 * CHAIN_BODY
                    v.wait_ge(v_done, l * (BODIES * 2 * TOPK) + t * (HEADS * TOPK) + (HEADS * TOPK + SLOTS))
                    pause(v)
                    own.link(v.tensor_copy(h_sb[:, ds(t, 1)].rearrange("p a k c -> p (a k c)"), ps[:, 6:8, :].rearrange("p b c -> p (b c)")))
                    own.link(v.memset(ps[:, 6:8, :], 0.0), to=CHAIN_TILE - 1)
                    v.sem_inc(y_zero, 1)
                own.base, own.n = outer, p0 + NT * CHAIN_TILE

                for t in range(NT):
                    u = f"yn{t}"
                    wait_unit(v, l, u)
                    src = both(u).rearrange("p (k c) -> p k c", c=P)
                    s = 0 if t < NL else 1
                    for k in range(KD):
                        op = v.scalar_tensor_tensor(x_sb[:, t, k, :], src[:, k, :], mod[:, 40 + k, s:s + 1], x_sb[:, t, k, :], ALU.mult, ALU.add)
                        if k < KD - 1:
                            own.tick(op)
                    op.then_inc(free[pair(u)], 1)
                for t in range(2, NT):
                    wait_free(v, l, f"yn{t}", 1)
                own.link(v.tensor_copy(st[:, 23:24], st[:, 16:17]), to=CHAIN_LAYER)
                v.sem_inc(x_ready, 1)

        @block.tensor
        def _(pe):
            pe.wait_ge(csil_ok, 1)
            pe.wait_ge(pool_own, 8)

            def project(u, l, src, c):
                wait_chunk(pe, l, c)
                wait_free(pe, l, u)
                for k in range(KD):
                    for s in range(2):
                        mm = pe.matmul(ps[:, 2 * pair(u) + s, 0:TOK // 2], wring[:, c % RING, k * P:(k + 1) * P],
                                       src(k)[:, :, s, :], start=(k == 0), stop=(k == KD - 1))
                mm.then_inc(w_done[c % RING], 1)

            def h_in(k):
                return split_half(h_sb[:, :, k, :])

            def half_sums(u, parts):
                for i, x in enumerate(parts):
                    for s in range(2):
                        mm = pe.matmul(ps[:, 2 * pair(u) + s, 0:TOK // 2], ones[:], x[:, :, s, :],
                                       start=(i == 0), stop=(i == len(parts) - 1))
                mm.then_inc(ready, 1)

            def ones_sum(u, l, parts0, parts1):
                b0, b1 = banks(u)
                for i, x in enumerate(parts0):
                    pe.matmul(b0, ones[:], x, start=(i == 0), stop=(i == len(parts0) - 1))
                for i, x in enumerate(parts1):
                    mm = pe.matmul(b1, ones[:], x, start=(i == 0), stop=(i == len(parts1) - 1))
                mm.then_inc(ready, 1)

            def rms(which, l):
                u = f"rms{which}"
                wait_free(pe, l, u)
                wait_count(pe, sq_ready, l, 2 * NT, NT * which)
                half_sums(u, [split_half(sq[:, :, k, :]) for k in range(KD)])

            def token_units(name, l, c0):
                for t in range(NT):
                    u = f"{name}{t}"
                    wait_free(pe, l, u)
                    for q in range(4):
                        if t == 0:
                            wait_chunk(pe, l, c0 + q)
                        for kk in range(2):
                            k = 2 * q + kk
                            mm = pe.matmul(banks(u)[0], h_sb[:, t, k, :], wring[:, (c0 + q) % RING, kk * 512:(kk + 1) * 512],
                                           start=(k == 0), stop=(k == KD - 1))
                        if t == NT - 1:
                            mm.then_inc(w_done[(c0 + q) % RING], 1)
                    if t < NT - 1:
                        mm.then_inc(ready, 1)
                    yield u

            with pe.Fori(0, DEPTH) as l:
                rms(1, l)
                pause(pe)
                with pe.Fori(0, 4) as it:
                    for b in range(3):
                        pr = (b + 1) % 3
                        pe.wait_ge(free[pr], l * TURNS + it + (1 + (b + 1) // 3))
                        for q in range(4):
                            c = 4 * b + q
                            wait_chunk(pe, l, c, it * 2)
                            for kk in range(2):
                                k = 2 * q + kk
                                mm = pe.matmul(ps[0:2, 2 * pr, :], csil[:, k, :], wring[:, c % RING, kk * 512:(kk + 1) * 512],
                                               start=(k == 0), stop=(k == KD - 1))
                            mm.then_inc(w_done[c % RING], 1)
                for b in range(3):
                    wait_free(pe, l, f"ada{9 + b}", 1)
                for c in range(48):
                    mm = pe.matmul(ps[:, 2 * pair("mod"), 2 * c:2 * c + 2], modrow[:, c * P:(c + 1) * P], ident[0:2, 0:2],
                                   start=True, stop=True)
                mm.then_inc(ready, 1)

                wait_count(pe, h_ready, l, 2, 1)
                for c in range(4):
                    project(f"cb{c}", l, h_in, CHUNK_OF[f"cb{c}"])
                    project(f"ca{c}", l, h_in, CHUNK_OF[f"ca{c}"])
                for g in range(4):
                    project(f"pl{g}", l, h_in, CHUNK_OF[f"pl{g}"])
                for i, name in enumerate(("dv", "nv")):
                    for _u in token_units(name, l, C_V + 4 * i):
                        pass

                def qk_units():
                    for i, b in enumerate(("dq", "dk", "nq", "nk")):
                        yield from token_units(b, l, C_QK + 4 * i)

                def qk_transpose(n):
                    wait_count(pe, qk_fin, l, 20, n + 1)
                    if n >= 2:
                        wait_count(pe, qk_evac, l, 20, n - 1)
                    qn = at(T, 1024 + (n % 2) * 512, 4, P)
                    for h in range(4):
                        mm = pe.transpose(ps[:, 6 + n % 2, h * P:(h + 1) * P], qn[:, h, :], ident[:])
                    mm.then_inc(qk_tr, 1)

                for n, _u in enumerate(qk_units()):
                    if n >= 2:
                        qk_transpose(n - 2)
                for n in range(len(QK) - 2, len(QK)):
                    qk_transpose(n)

                wait_free(pe, l, "lnm")
                wait_count(pe, conv_done, l, 1, 1)
                ones_sum("lnm", l, [acc[:, c, 0:LAT] for c in range(4)], [acc[:, c, SPAN - SEQ:SPAN] for c in range(4)])
                wait_free(pe, l, "lnv")
                wait_count(pe, csq, l, 4, 4)
                csqv = at(T, 0, 4, TOK)
                ones_sum("lnv", l, [csqv[:, c, 0:LAT] for c in range(4)], [csqv[:, c, LAT:TOK] for c in range(4)])
                wait_count(pe, pool_in, l * 16, 1, 16)
                for g in range(4):
                    u = f"pw{g}"
                    wait_free(pe, l, u)
                    wait_count(pe, pool_d, l, 4, g + 1)
                    for s in range(2):
                        mm = pe.matmul(ps[:, 2 * pair(u) + s, 0:TOK // 2], pw_sb[:, g, :], by_half(yT[:, g, :])[:, :, s, :],
                                       start=True, stop=True)
                    mm.then_inc(ready, 1)

                def keys(kind, h, i, t):
                    if kind == "diff":
                        lo, qT, kT, c = 64 * i, dqT, dkT, h
                    else:
                        lo, qT, kT, c = 64 * (h % 2), nqT, nkT, h // 2
                    q = qT[lo:lo + 64, c, t * P:(t + 1) * P]
                    k = kT[lo:lo + 64, c, :]
                    if t == NL:
                        return q, [(k[:, LAT:TOK], SEQ)]
                    if kind == "diff":
                        return q, [(k[:, 0:LAT], LAT), (k[:, TOK:TOK + PAST], PAST)]
                    win = k[:, 0:LAT].rearrange("p (r c) -> p r c", c=GRID_W)[:, :, COL0[t]:COL0[t] + KB]
                    return q, [(win, ROWS * KB), (k[:, TOK:TOK + PAST], PAST)]

                def values(kind, h, t):
                    if kind == "diff":
                        c = slice(h * P, (h + 1) * P)
                        return [dv[:, NL, c]] if t == NL else [dv[:, i, c] for i in (0, 1, 2, 3, 5)]
                    c = slice((h // 2) * P, (h // 2 + 1) * P)
                    return [nv[:, 0, c]] if t == NL else [vwin[:, 2 * t, c], vwin[:, 2 * t + 1, c], nv[:, 1, c]]

                def job_scores(n):
                    kind, h, t = JOBS[n]
                    for i in range(MAPS[n]):
                        m = MAP0[n] + i
                        if m >= 2:
                            wait_count(pe, exp_done, l, NMAPS, m - 1)
                        q, ks = keys(kind, h, i, t)
                        start = 0
                        for k, width in ks:
                            b = 2 * (m % 2) + start // 512
                            mm = pe.matmul(ps[:, b, start % 512:start % 512 + width], q, k, start=True, stop=True, skip_group_check=True)
                            start += width
                        mm.then_inc(s_ready, 1)

                for u in ("pw1", "pw2", "pw3"):
                    wait_free(pe, l, u, 1)
                wait_count(pe, qk_evac, l, 20, 20)
                wait_count(pe, ctx_in, l * 16, 4, 64)
                wait_count(pe, y_conv, l, 1, 1)

                def job_values(n):
                    kind, h, t = JOBS[n]
                    vs = values(kind, h, t)
                    if kind == "nat" and h == 0 and t == 0:
                        wait_count(pe, vb_in, l * 16, 32, 512)
                    wait_count(pe, pt_evac, l, NJOBS, n + 1)
                    if n >= 2:
                        wait_count(pe, o_evac, l, NJOBS, n - 1)
                    pt = at(T, 2560, 5, P)
                    for i, x in enumerate(vs):
                        mm = pe.matmul(ps[:, 6 + n % 2, 0:P], x, pt[:, i, :], start=(i == 0), stop=(i == len(vs) - 1))
                    mm.then_inc(o_ready, 1)

                job_scores(0)
                for n, (kind, h, t) in enumerate(JOBS):
                    if n + 1 < NJOBS:
                        job_scores(n + 1)
                    if n:
                        job_values(n - 1)
                    wait_count(pe, pd_ready, l, NJOBS, n + 1)
                    Pn = at(T, (n % 2) * 1280, TOK)
                    for i in range(job_width(kind, t) // P):
                        mm = pe.transpose(ps[:, 4 + i // 4, (i % 4) * P:(i % 4 + 1) * P], Pn[:, i * P:(i + 1) * P], ident[:])
                    mm.then_inc(t_ready, 1)
                job_values(NJOBS - 1)

                for h in range(4):
                    u = f"dr{h}"
                    wait_free(pe, l, u)
                    wait_count(pe, dsq, l, 4, h + 1)
                    r = at(T, (h % 2) * TOK, TOK)
                    half_sums(u, [by_half(r)])

                for h in range(1, 4):
                    wait_free(pe, l, f"dr{h}", 1)
                wait_count(pe, y_diff, l, 4, 4)
                pause(pe)
                with pe.Fori(0, 4) as dp:
                    for n in range(8):
                        i, dd = n // 2, n % 2
                        c = C_MERGE + 3 * i + dd
                        wait_chunk(pe, l, c, dp * 2)
                        pe.wait_ge(br_evac, l * 32 + dp * 8 + (n + 1))
                        g = 2 * (n % 2)
                        for k in range(KD):
                            wk = wring[:, c % RING, k * P:(k + 1) * P]
                            for s in range(2):
                                mm = pe.matmul(ps[:, g + s, 0:TOK // 2], wk, h_in(k)[:, :, s, :], start=(k == 0), stop=(k == KD - 1))
                        mm.then_inc(w_done[c % RING], 1)
                        c = C_MERGE + 3 * i + 2
                        wait_chunk(pe, l, c, dp * 2)
                        for k in range(4):
                            wk = wring[:, c % RING, (dd * 4 + k) * P:(dd * 4 + k + 1) * P]
                            for s in range(2):
                                mm = pe.matmul(ps[:, 4 + g + s, 0:TOK // 2], wk, by_half(yT[:, 4 * i + k, :])[:, :, s, :], start=(k == 0), stop=(k == 3))
                        mm.then_inc(w_done[c % RING] if dd else br_ready, 1)

                wait_count(pe, merged_ok, l, 4, 4)
                for d in range(KD):
                    project(f"o{d}", l, lambda k: by_half(merged[:, k, :]), C_OUT + d)
                rms(2, l)

                wait_count(pe, h_ready, l, 2, 2)
                wait_count(pe, subk_in, l * 16, 1, 16)

                def peer_scores(n):
                    u = f"s{n}"
                    wait_free(pe, l, f"q{n}", 1)
                    wait_free(pe, l, u)
                    b0, b1 = banks(u)
                    for t in range(NT):
                        o = b0[:, t * P:(t + 1) * P] if t < NL else b1
                        mm = pe.matmul(o, qst[:, n % 2, t * P:(t + 1) * P], sk[:, n, :], start=True, stop=True)
                    mm.then_inc(ready, 1)

                for n in range(16):
                    project(f"q{n}", l, h_in, C_QUERY + n)
                    if n:
                        peer_scores(n - 1)
                peer_scores(15)

                def turn_tiles(name):
                    for t in range(NT):
                        u = f"{name}{t}"
                        wait_free(pe, l, u)
                        for k in range(KD):
                            mm = pe.transpose(both(u)[:, k * P:(k + 1) * P], h_sb[:, t, k, :], ident[:])
                        mm.then_inc(ready, 1)

                turn_tiles("hn")

                pause(pe)
                with pe.Fori(0, NT) as t:
                    pe.wait_ge(y_zero, l * (NT + 1) + t + 1)
                    pause(pe)
                    with pe.Fori(0, HEADS // 2) as q:
                        for n in range(2 * GRPS):
                            pe.wait_ge(dg_ready, l * (BODIES * 2 * GRPS) + t * (HEADS * GRPS) + q * (2 * GRPS) + (n + 1))
                            for e in range(GRP):
                                s = (n * GRP + e) % SLOTS
                                for c in range(2):
                                    mm = pe.matmul(ps[:, 6 + c, :], dg[:, n % 2, e, :], rows[:, s, D + c * 512:D + (c + 1) * 512],
                                                   start=False, stop=False, skip_group_check=True)
                                mm.then_inc(v_done, 1)
                pe.wait_ge(y_zero, l * (NT + 1) + NT + 1)
                turn_tiles("yn")

            pe.wait_ge(x_ready, 2 * DEPTH + 1)
            for t in range(NT):
                pe.wait_ge(free[t % 3], DEPTH * TURNS + t // 3 + 1)
                b = 2 * (t % 3)
                for k in range(KD):
                    mm = pe.transpose(ps[:, b + k // 4, (k % 4) * P:(k % 4 + 1) * P], x_sb[:, t, k, :], ident[:])
                mm.then_inc(ready, 1)


def _col_chunks(m):
    n = m.shape[1] // P
    return m.reshape(KD, P, n, P).transpose(2, 1, 0, 3).reshape(n, P, 1024)


def _row_chunks(m):
    n = m.shape[1] // 512
    return m.reshape(4, 2, P, n, 512).transpose(3, 0, 2, 1, 4).reshape(4 * n, P, 1024)


def _chans(v):
    return v.reshape(-1, P).T


def kernel(**inputs):
    import concourse.bacc as bacc
    from concourse.bass_utils import run_bass_kernel_spmd

    a = {k: np.asarray(x) for k, x in inputs.items()}
    order = (0, 2, 1, 3)
    stream, small, rowg, lamrow = [], [], [], []
    for l in range(DEPTH):
        wi = a["w_in"][l]
        parts = [_row_chunks(a["w_ada"][l])]
        ca, cb = _col_chunks(wi[:, 2048:2560]), _col_chunks(wi[:, 2560:3072])
        for c in range(4):
            parts += [cb[c:c + 1], ca[c:c + 1]]
        parts.append(_col_chunks(wi[:, 0:512]))
        for s in (4096, 1536, 3072, 3584, 512, 1024):
            parts.append(_row_chunks(wi[:, s:s + 512]))
        wg = _col_chunks(a["w_gate"][l])
        wb = a["w_branch"][l].reshape(4, 4, P, 4, 2, P)
        for dp in range(4):
            for i in order:
                parts += [wg[8 * i + 2 * dp:8 * i + 2 * dp + 2], wb[i, :, :, dp].transpose(1, 2, 0, 3).reshape(1, P, 1024)]
        parts += [_col_chunks(a["w_out"][l]), _col_chunks(a["peer_w_query"][l])]
        stream.append(np.concatenate(parts))
        small.append(np.concatenate([
            _chans(a["b_ada"][l]), _chans(a["norm1_g"][l]), _chans(a["norm2_g"][l]), _chans(a["pool_scale"][l]),
            a["conv_w"][l].reshape(CONV_W, 4, P).transpose(2, 1, 0).reshape(P, 4 * CONV_W),
            _chans(a["conv_b"][l]), _chans(a["conv_ln_g"][l]), _chans(a["conv_ln_b"][l]), _chans(a["diff_subln_g"][l]),
            _chans(a["b_gate"][l].reshape(4, D)[list(order)]),
        ], axis=1))
        rowg.append(np.broadcast_to(np.concatenate([a[n][l] for n in ("nat_q_g", "nat_k_g", "diff_q_g", "diff_k_g")]), (P, 256)))
        lamrow.append(np.broadcast_to(a["diff_lambda_p"][l].reshape(256), (P, 256)))

    lam_init = [0.8 - 0.6 * float(np.exp(-0.3 * l)) for l in range(DEPTH)]
    clay = np.zeros((DEPTH, P, 4), np.float32)
    for l in range(DEPTH):
        clay[l, :, 0:3] = (lam_init[l], 1 - lam_init[l], l * NEXP)
    freqs = (np.float32(10000.0) ** (-np.arange(16, dtype=np.float32) / np.float32(16))).astype(np.float32)
    tok = np.arange(LAT)
    rope = np.zeros((P, NL, 2, 64), np.float32)
    for axis, pos in enumerate((tok // GRID_W, tok % GRID_W)):
        ang = pos.astype(np.float32)[:, None] * freqs
        for half in range(2):
            o = axis * 32 + half * 16
            rope[:, :, 0, o:o + 16] = np.cos(ang).reshape(NL, P, 16).transpose(1, 0, 2)
            rope[:, :, 1, o:o + 16] = (np.sin(ang) * (1 if half else -1)).reshape(NL, P, 16).transpose(1, 0, 2)
    edge = np.zeros((P, 4, 16), np.float32)
    for g, win in enumerate(POOL_WINDOWS):
        for i in range(8):
            edge[:, g, i] = 1.0 / (i + win - win // 2 - max(i - win // 2, 0))
            j = SEQ - 8 + i
            edge[:, g, 8 + i] = 1.0 / (min(j + win - win // 2, SEQ) - (j - win // 2))
    qcol = (np.arange(NJ)[:, None] * QB + np.arange(QB))
    kcol = np.array(COL0)[:, None] + np.arange(KB)
    wstart = np.clip(qcol - WIN_C // 2, 0, GRID_W - WIN_C)
    rel = kcol[:, None, :] - wstart[:, :, None]
    valid = (rel >= 0) & (rel < WIN_C)
    m = np.where(valid, 0.0, NEG_INF).astype(np.float32).transpose(1, 0, 2)
    mask = np.tile(m, (ROWS, 1, 1))
    drow = np.arange(ROWS)[None, :] - np.arange(ROWS)[:, None] + WIN_R - 1
    dcol = np.clip(kcol[:, None, :] - qcol[:, :, None] + WIN_C - 1, 0, 2 * WIN_C - 2)
    rb = a["nat_rel_bias"][:, :, drow[:, None, None, :, None], dcol.transpose(1, 0, 2)[None, :, :, None, :]]
    bias = rb.reshape(DEPTH * 8, P, NJ, ROWS * KB)

    x = np.concatenate([a["x_sample"][0], a["x_prompt"][0]])
    arrays = {
        "xT": x.reshape(NT, P, KD, P).transpose(3, 0, 2, 1),
        "cT": np.stack([_chans(a["c"][0]), _chans(a["c_ctx"])], axis=2),
        "w": np.concatenate(stream), "small": np.stack(small), "rowg": np.concatenate(rowg), "lamrow": np.concatenate(lamrow),
        "clay": clay, "poolw": a["pool_w"].transpose(0, 2, 1, 3),
        "subk": a["peer_sub_keys"].reshape(DEPTH, 16, NKEYS, P).transpose(0, 3, 1, 2),
        "rope": rope, "edge": edge, "mask": mask, "bias": bias,
        "ckn": a["cache_nat_k"][0].reshape(DEPTH, PAST, 4, P).transpose(0, 3, 2, 1),
        "ckd": a["cache_diff_k"][0].reshape(DEPTH, PAST, 4, P).transpose(0, 3, 2, 1),
        "cvn": a["cache_nat_v"][0].reshape(DEPTH, PAST, BW), "cvd": a["cache_diff_v"][0].reshape(DEPTH, PAST, BW),
        "experts": np.concatenate([a["peer_u"].reshape(-1, D), a["peer_v"].reshape(-1, D)], axis=1),
    }
    arrays = {k: np.ascontiguousarray(v) for k, v in arrays.items()}
    outs = {"y_prompt": (SEQ, D), "y_sample": (LAT, D), "o_nk": (DEPTH * SEQ, BW), "o_nv": (DEPTH * SEQ, BW),
            "o_dk": (DEPTH * SEQ, BW), "o_dv": (DEPTH * SEQ, BW)}
    nc = bacc.Bacc("TRN2", target_bir_lowering=False, num_devices=1)
    args = {k: nc.dram_tensor(k, v.shape, F32, kind="ExternalInput").ap() for k, v in arrays.items()}
    args |= {k: nc.dram_tensor(k, s, F32, kind="ExternalOutput").ap() for k, s in outs.items()}
    backbone(nc, **args)
    r = run_bass_kernel_spmd(nc, [arrays], core_ids=[0]).results[0]
    return (r["y_prompt"].reshape(1, SEQ, D), r["y_sample"].reshape(1, LAT, D),
            r["o_nk"].reshape(1, DEPTH, SEQ, 8, 64), r["o_nv"].reshape(1, DEPTH, SEQ, 8, 64),
            r["o_dk"].reshape(1, DEPTH, SEQ, 4, 2, 64), r["o_dv"].reshape(1, DEPTH, SEQ, 4, 128))
```

```python
from contextlib import ExitStack

import concourse.bass as bass
import numpy as np
from concourse import mybir

F32 = mybir.dt.float32
U32 = mybir.dt.uint32
ALU = mybir.AluOpType
ACT = mybir.ActivationFunctionType
AX_X = mybir.AxisListType.X
ds = bass.ds

P = 128
D = 1024
KD = D // P
SEQ, LAT, PAST = 128, 512, 128
TOK = LAT + SEQ
NT = TOK // P
NL = LAT // P
HT = P // 2
DEPTH = 2
EPS = 1e-6
NEG_INF = -1e30
GRID_W, ROWS = 64, 8
NJ, QB, KB = 4, 16, 32
WIN_C, WIN_R = 16, 8
COL0 = [min(max(j * QB - WIN_C // 2, 0), GRID_W - KB) for j in range(NJ)]
CONV_W = 31
POOL_WINDOWS = (2, 4, 8, 16)
PAD = 16
LAT0, CTX0 = PAD, 2 * PAD + LAT
PADDED = 3 * PAD + TOK
SPAN = CTX0 + SEQ - LAT0
BW = 512
HEADS, NKEYS, TOPK = 8, 128, 16
NEXP = NKEYS * NKEYS
LOWEST = -3.0e38

RING = 6
C_ADA, C_CONV, C_POOL, C_V, C_QK, C_MERGE, C_OUT, C_QUERY, NCHUNK = 0, 48, 56, 60, 68, 84, 132, 140, 156
USES = NCHUNK // RING

S_BADA, S_N1, S_N2, S_PSC, S_CW, S_CB, S_LG, S_LB, S_SUB, S_BG = 0, 48, 56, 64, 68, 192, 196, 200, 204, 205
NSMALL = 237

UNITS = [f"ada{n}" for n in range(6)] + ["rms1"] + [f"ada{n}" for n in range(6, 12)]
for _c in range(4):
    UNITS += [f"cb{_c}", f"ca{_c}"]
UNITS += ["mod"] + [f"pl{g}" for g in range(4)]
UNITS += [f"dv{t}" for t in range(NT)] + [f"nv{t}" for t in range(NT)]
QK = [(b, t) for b in ("dq", "dk", "nq", "nk") for t in range(NT)]
LNM_AT, LNV_AT = 8, 14


def with_norm(keep):
    out = []
    for n, (b, t) in enumerate(QK):
        if keep(t):
            out.append(f"{b}{t}")
        out += ["lnm"] * (n == LNM_AT) + ["lnv"] * (n == LNV_AT)
    return out


UNITS += with_norm(lambda t: True)
UNITS += [f"pw{g}" for g in range(4)] + [f"dr{h}" for h in range(4)]
UNITS += [f"o{d}" for d in range(KD)] + ["rms2", "q0"]
for _n in range(1, 16):
    UNITS += [f"q{_n}", f"s{_n - 1}"]
UNITS += ["s15"] + [f"hn{t}" for t in range(NT)] + [f"yn{t}" for t in range(NT)]
UNIT = {u: n for n, u in enumerate(UNITS)}
TURNS = len(UNITS) // 3
assert TURNS * 3 == len(UNITS)
FIN0 = DEPTH * len(UNITS)

READY = ["rms1", "mod"] + [f"dv{t}" for t in range(NT - 1)] + [f"nv{t}" for t in range(NT - 1)]
READY += with_norm(lambda t: t < NT - 1)
READY += [f"pw{g}" for g in range(4)] + [f"dr{h}" for h in range(4)] + ["rms2"]
READY += [f"s{n}" for n in range(16)] + [f"hn{t}" for t in range(NT)] + [f"yn{t}" for t in range(NT)]
READY_AT = {u: n for n, u in enumerate(READY)}
CHUNK_OF = {f"cb{c}": C_CONV + 2 * i for i, c in enumerate(range(4))}
CHUNK_OF |= {f"ca{c}": C_CONV + 2 * i + 1 for i, c in enumerate(range(4))}
CHUNK_OF |= {f"pl{g}": C_POOL + g for g in range(4)}
CHUNK_OF |= {f"dv{NT - 1}": C_V + 3, f"nv{NT - 1}": C_V + 7}
CHUNK_OF |= {f"{b}{NT - 1}": C_QK + 4 * i + 3 for i, b in enumerate(("dq", "dk", "nq", "nk"))}
CHUNK_OF |= {f"o{d}": C_OUT + d for d in range(KD)} | {f"q{n}": C_QUERY + n for n in range(16)}

JOBS = [("diff", h, t) for h in range(4) for t in range(NT)]
JOBS += [("nat", h, j) for h in range(8) for j in range(NT)]
NJOBS = len(JOBS)
MAPS = [2 if kind == "diff" else 1 for kind, _, _ in JOBS]
MAP0 = [sum(MAPS[:n]) for n in range(NJOBS)]
NMAPS = sum(MAPS)
MAP_JOB = [(n, i) for n in range(NJOBS) for i in range(MAPS[n])]


def maps_at(n, ahead):
    last = min(MAP0[n] + MAPS[n] - 1 + ahead, NMAPS - 1)
    first = 0 if n == 0 else min(MAP0[n] - 1 + ahead, NMAPS - 1) + 1
    return range(first, last + 1)

GRP = 4
SLOTS = 2 * GRP
GRPS = TOPK // GRP
BODIES = NT * HEADS // 2
CHAIN_LAYER = 4096
CHAIN_BODY = 128
CHAIN_TILE = 4 * CHAIN_BODY + 1


class Chain:

    def __init__(self, eng, sem):
        self.eng, self.sem, self.base, self.n = eng, sem, 0, 0

    def tick(self, ins, to=None):
        step = 1 if to is None else to - self.n
        assert step > 0
        ins.then_inc(self.sem, step)
        self.n += step

    def wait(self):
        self.eng.wait_ge(self.sem, self.base + self.n)

    def link(self, ins, to=None):
        self.tick(ins, to)
        self.wait()


def backbone(nc, xT, cT, w, small, rowg, lamrow, clay, poolw, subk, rope, edge, mask, bias, ckn, ckd,
             cvn, cvd, experts, y_prompt, y_sample, o_nk, o_nv, o_dk, o_dv):
    with ExitStack() as cx:
        def sb(name, shape, dt=F32):
            return cx.enter_context(nc.sbuf_tensor(name, shape, dt))

        def sem(name):
            return cx.enter_context(nc.semaphore(name))

        vscr = nc.dram_tensor("v_scratch", (LAT, BW), F32, kind="Internal").ap()

        x_sb = sb("x_sb", [P, NT, KD, P])
        h_sb = sb("h_sb", [P, NT, KD, P])
        wring = sb("wring", [P, RING, 1024])
        arena = sb("arena", [P, 29696])
        bsb = sb("bsb", [P, 2064])
        T = sb("T", [P, 3200])
        sm = sb("sm", [P, NSMALL])
        rg = sb("rg", [P, 256])
        cl = sb("cl", [P, 4])
        mod = sb("mod_sb", [P, 48, 2])
        amp = sb("amp", [P, 2, KD, 2])
        ident = sb("ident", [P, P])
        ones = sb("ones", [P, P])
        rp = sb("rp", [P, NL, 2, 64])
        ed = sb("ed", [P, 4, 16])
        mk = sb("mk", [P, NJ, KB])
        csil = sb("csil", [P, KD, 2])
        lam = sb("lam", [P, 8])
        st = sb("st", [P, 48])
        ps = cx.enter_context(nc.psum_tensor("ps", [P, 8, 512], F32))

        def at(tensor, start, *shape):
            n = int(np.prod(shape))
            v = tensor[:, start:start + n]
            if len(shape) == 1:
                return v
            names = "abcd"[:len(shape)]
            return v.rearrange(f"p ({' '.join(names)}) -> p {' '.join(names)}", **dict(zip(names, shape)))

        yT = at(arena, 0, 16, TOK)
        acc = at(arena, 4 * TOK, 4, SPAN)
        U = at(arena, 4 * TOK + 4 * SPAN, 4, PADDED)
        csqv = at(arena, 4 * TOK + 4 * SPAN, 4, TOK)
        vst = at(arena, 16 * TOK - 1024, 2, BW)
        pw_sb = at(arena, 16 * TOK - 1536, 4, P)
        A0, B0 = 16 * TOK, 16 * TOK + 8704
        dqT, dkT, dv = at(arena, A0, 4, TOK), at(arena, A0 + 2560, 4, 768), at(arena, A0 + 5632, 6, BW)
        nqT, nkT = at(arena, B0, 4, TOK), at(arena, B0 + 2560, 4, 768)
        vwin, nv = at(arena, B0 + 5632, 8, BW), at(arena, B0 + 5632 + 4096, 2, BW)
        MOD_ROW, MOD_STEP = A0 + 5632, 3072
        sq = at(arena, A0, NT, KD, P)
        droots = at(arena, B0 + 4 * TOK, 4, TOK)
        sq2 = at(arena, B0 + 4 * TOK, KD, NT, P)
        xs = at(arena, 0, NT, KD, P)
        merged = at(arena, A0, KD, TOK)
        gt = at(arena, B0, 2, TOK)
        prod = at(arena, B0 + 2 * TOK, 2, TOK)
        rstd = at(T, 0, TOK)
        scores = at(arena, 0, NT * 16 + 2, NKEYS)
        SC_END = (NT * 16 + 2) * NKEYS
        rows = at(arena, SC_END, SLOTS, 2 * D)
        sk = at(arena, SC_END + SLOTS * 2 * D, 16, NKEYS)
        qst = at(T, 0, 2, TOK)
        ROUTE = 2 * TOK
        sc = at(T, ROUTE, 2, NKEYS)
        screp = at(T, ROUTE + 256, 2, NKEYS)
        cand = at(T, ROUTE + 512, TOPK, TOPK)
        crep = at(T, ROUTE + 768, 256)
        hot = at(T, ROUTE + 1024, 2, TOPK, TOPK)
        top = at(T, ROUTE + 1536, 2, TOPK)
        topf = at(T, ROUTE + 1568, 2, TOPK)
        csc = at(T, ROUTE + 1600, 2, TOPK)
        abf = at(T, ROUTE + 1632, 2, TOPK)
        sel = at(T, ROUTE + 1664, 2, TOPK)
        ef = at(T, ROUTE + 1696, TOPK)
        gate = at(T, ROUTE + 1712, 2, TOPK)
        dots = at(T, ROUTE + 1744, 2, TOPK)
        gel = at(T, ROUTE + 1776, 2, TOPK)
        wgt = at(T, ROUTE + 1808, 2, TOPK)
        iota = at(T, ROUTE + 1840, TOPK)
        topi = sb("topi", [P, 2, TOPK], U32)
        ci = sb("ci", [P, 3, TOPK], U32)
        eidx = sb("eidx", [P, 2, TOPK], U32)
        iota_i = sb("iota_i", [P, TOPK], mybir.dt.int32)
        dg = at(bsb, 0, 2, GRP, P)

        w_load = [sem(f"w_load{i}") for i in range(RING)]
        w_done = [sem(f"w_done{i}") for i in range(RING)]
        free = [sem(f"pair_free{i}") for i in range(3)]
        ready = sem("unit_ready")
        const_in, ctab = sem("const_in"), sem("ctab")
        params, lam_in, pool_in, ctx_in, subk_in = [sem(n) for n in ("params", "lam_in", "pool_in", "ctx_in", "subk_in")]
        csil_ok, lam_exp = sem("csil_ok"), sem("lam_exp")
        lam_sum = sem("lam_sum")
        mod_first = sem("mod_first")
        x_ready, sq_ready, root, h_ready = sem("x_ready"), sem("sq_ready"), sem("root"), sem("h_ready")
        u_ready, conv_pool, conv_done, pool_d = sem("u_ready"), sem("conv_pool"), sem("conv_done"), sem("pool_d")
        vb_out, vb_in, state_out = [sem(f"vb_out{i}") for i in range(2)], sem("vb_in"), sem("state_out")
        qk_sq, qk_ms, qk_root, qk_fin, qk_evac, qk_tr = [sem(n) for n in ("qk_sq", "qk_ms", "qk_root", "qk_fin", "qk_evac", "qk_tr")]
        cen_ok, csq, cms, croot, cnorm, y_conv = [sem(n) for n in ("cen_ok", "csq", "cms", "croot", "cnorm", "y_conv")]
        bias_in, bias_ok = [sem(f"bias_in{i}") for i in range(2)], sem("bias_ok")
        s_ready, m_ready, exp_done, pd_ready, t_ready, pt_evac, o_ready, o_evac = [
            sem(n) for n in ("s_ready", "m_ready", "exp_done", "pd_ready", "t_ready", "pt_evac", "o_ready", "o_evac")]
        dsq, droot, y_diff = sem("dsq"), sem("droot"), sem("y_diff")
        br_ready, gate_evac, br_evac, merged_ok = sem("br_ready"), sem("gate_evac"), sem("br_evac"), sem("merged_ok")
        gath = [sem(f"gath{i}") for i in range(SLOTS)]
        idx_ready, top_ready, gexp, dot, gelu_ok, dg_ready, v_done, y_zero, y_taken = [
            sem(n) for n in ("idx_ready", "top_ready", "gexp", "dot", "gelu_ok", "dg_ready", "v_done", "y_zero", "y_taken")]
        dve_own, act_own, pool_own = sem("dve_own"), sem("act_own"), sem("pool_own")
        out_done = sem("out_done")

        def pair(u):
            return UNIT[u] % 3

        def wait_free(eng, l, u, more=0):
            eng.wait_ge(free[pair(u)], l * TURNS + (UNIT[u] // 3 + 1) + more)

        def wait_unit(eng, l, u):
            if u in READY_AT:
                eng.wait_ge(ready, l * len(READY) + (READY_AT[u] + 1))
            else:
                eng.wait_ge(w_done[CHUNK_OF[u] % RING], l * USES + (CHUNK_OF[u] // RING + 1))

        def wait_chunk(eng, l, c, turn=0):
            eng.wait_ge(w_load[c % RING], (l * USES + (c // RING + 1) + turn) * 16)

        def wait_count(eng, s, l, per_layer, n):
            eng.wait_ge(s, l * per_layer + n)

        def pause(eng):
            eng.nop(nofuse=True)

        def banks(u):
            b = 2 * pair(u)
            return ps[:, b, :], ps[:, b + 1, 0:P]

        def halves(u):
            b = 2 * pair(u)
            return halves_at(b)

        def halves_at(b):
            return ps[:, b:b + 2, 0:TOK // 2].rearrange("p s (t c) -> p t s c", c=HT)

        def by_half(ap):
            return ap.rearrange("p (t s c) -> p t s c", s=2, c=HT)

        def split_half(ap3):
            return ap3.rearrange("p t (s c) -> p t s c", c=HT)

        def both(u):
            b = 2 * pair(u)
            return ps[:, b:b + 2, :].rearrange("p b c -> p (b c)")

        def tile4(ap):
            return ap.rearrange("p (t c) -> p t c", c=P)

        def job_width(kind, t):
            return SEQ if t == NL else (TOK if kind == "diff" else ROWS * KB + PAST)

        def map_banks(m):
            b = 2 * (m % 2)
            return ps[:, b:b + 2, :].rearrange("p b c -> p (b c)")

        def job_out(act, l, n, own, wait_count):
            kind, h, t = JOBS[n]
            wait_count(act, o_ready, l, NJOBS, n + 1)
            src = ps[:, 6 + n % 2, 0:P]
            if kind == "diff":
                op = act.activation(yT[:, 12 + h, t * P:(t + 1) * P], src, ACT.Copy)
            else:
                lo = 64 * (h % 2)
                row = yT[lo:lo + 64, 8 + h // 2, :]
                if t == NL:
                    op = act.activation(row[:, LAT:TOK], src[lo:lo + 64, :], ACT.Copy)
                else:
                    dst = row[:, 0:LAT].rearrange("p (r c) -> p r c", c=GRID_W)[:, :, t * QB:(t + 1) * QB]
                    op = act.activation(dst, src[lo:lo + 64, :].rearrange("p (r c) -> p r c", c=QB), ACT.Copy)
            op.then_inc(o_evac, 1)

        block = cx.enter_context(nc.Block())

        @block.sync
        def _(sp):
            for s in range(RING):
                sp.dma_start(wring[:, s, :], w[s]).then_inc(w_load[s], 16)
            with sp.Fori(1, DEPTH * USES) as turn:
                for s in range(RING):
                    sp.wait_ge(w_done[s], turn)
                    pause(sp)
                    sp.dma_start(wring[:, s, :], w[ds(turn * RING + s, 1)].rearrange("a p n -> (a p) n")).then_inc(w_load[s], 16)
            sp.wait_ge(out_done, 16 * NT)
            sp.wait_ge(state_out, 16 * 4 * DEPTH)

        @block.gpsimd
        def _(gp):
            own = Chain(gp, pool_own)
            gp.dma_start(x_sb[:], xT).then_inc(const_in, 16)
            gp.dma_start(csil[:], cT).then_inc(ctab, 16)
            gp.dma_start(rp[:], rope).then_inc(const_in, 16)
            gp.dma_start(ed[:], edge).then_inc(const_in, 16)
            gp.dma_start(mk[:], mask).then_inc(const_in, 16)
            own.link(gp.memset(ident[:], 0.0))
            own.link(gp.affine_select(out=ident[:], in_=ident[:], compare_op=ALU.not_equal, fill=1.0, base=0,
                                      pattern=[[-1, P]], channel_multiplier=1))
            own.link(gp.memset(ones[:], 1.0))
            gp.wait_ge(const_in, 64)
            own.tick(gp.iota(iota_i[:], pattern=[[1, TOPK]], base=0, channel_multiplier=0), to=8)

            with gp.Fori(0, DEPTH) as l:
                own.base, own.n = l * CHAIN_LAYER + 8, 0
                wait_count(gp, x_ready, l, 1, 1)
                pause(gp)
                gp.dma_start(sm[:], small[ds(l, 1)].rearrange("a p n -> (a p) n")).then_inc(params, 16)
                gp.dma_start(rg[:], rowg[ds(l * P, P)]).then_inc(params, 16)
                gp.dma_start(cl[:], clay[ds(l, 1)].rearrange("a p n -> (a p) n")).then_inc(params, 16)
                gp.dma_start(at(T, 640, 256), lamrow[ds(l * P, P)]).then_inc(lam_in, 16)
                for t in range(NT):
                    gp.tensor_tensor(sq[:, t], x_sb[:, t], x_sb[:, t], ALU.mult).then_inc(sq_ready, 1)
                wait_count(gp, h_ready, l, 2 * KD, KD)
                wait_count(gp, lam_sum, l, 1, 1)
                pause(gp)
                own.tick(gp.memset(U, 0.0))
                own.link(gp.memset(at(bsb, 0, 3, PADDED), 0.0))
                gp.dma_start(pw_sb, poolw[ds(l, 1)].rearrange("a p g c -> (a p) g c")).then_inc(pool_in, 16)
                gp.dma_start(dkT[:, :, TOK:TOK + PAST], ckd[ds(l, 1)].rearrange("a p h c -> (a p) h c")).then_inc(ctx_in, 16)
                gp.dma_start(nkT[:, :, TOK:TOK + PAST], ckn[ds(l, 1)].rearrange("a p h c -> (a p) h c")).then_inc(ctx_in, 16)
                gp.dma_start(dv[:, 5, :], cvd[ds(l, 1)].rearrange("a p c -> (a p) c")).then_inc(ctx_in, 16)
                gp.dma_start(nv[:, 1, :], cvn[ds(l, 1)].rearrange("a p c -> (a p) c")).then_inc(ctx_in, 16)
                gp.sem_inc(conv_pool, 1)

                u, sA, sB = (at(bsb, i * PADDED, PADDED) for i in range(3))
                for g, win in enumerate(POOL_WINDOWS):
                    wait_free(gp, l, f"pl{g}", 1)
                    pause(gp)
                    own.tick(gp.tensor_copy(u[:, LAT0:LAT0 + LAT], yT[:, g, 0:LAT]))
                    own.link(gp.tensor_copy(u[:, CTX0:CTX0 + SEQ], yT[:, g, LAT:TOK]))
                    src, dst, half = u, sA, 1
                    lo, hi = 1, PADDED
                    pause(gp)
                    own.link(gp.tensor_tensor(dst[:, lo:hi], src[:, lo - 1:hi - 1], src[:, lo:hi], ALU.add))
                    while 2 * half < win:
                        src, dst = dst, (sB if dst is sA else sA)
                        lo, hi = lo + half, hi - half
                        pause(gp)
                        own.link(gp.tensor_tensor(dst[:, lo:hi], src[:, lo - half:hi - half], src[:, lo + half:hi + half], ALU.add))
                        half *= 2
                    other = sB if dst is sA else sA
                    pause(gp)
                    own.link(gp.tensor_scalar(other[:, LAT0:LAT0 + SPAN], dst[:, LAT0:LAT0 + SPAN], 1.0 / win, None, ALU.mult))
                    for s in (LAT0, LAT0 + LAT - 8, CTX0, CTX0 + SEQ - 8):
                        e = 0 if s in (LAT0, CTX0) else 8
                        pause(gp)
                        own.tick(gp.tensor_tensor(other[:, s:s + 8], dst[:, s:s + 8], ed[:, g, e:e + 8], ALU.mult))
                    own.wait()
                    pause(gp)
                    own.tick(gp.tensor_tensor(yT[:, g, 0:LAT], other[:, LAT0:LAT0 + LAT], u[:, LAT0:LAT0 + LAT], ALU.subtract))
                    gp.tensor_tensor(yT[:, g, LAT:TOK], other[:, CTX0:CTX0 + SEQ], u[:, CTX0:CTX0 + SEQ], ALU.subtract).then_inc(pool_d, 1)
                    wait_count(gp, pool_d, l, 4, g + 1)

                for i in range(2):
                    wait_count(gp, vb_out[i], l * 16, 2, 32)
                pause(gp)
                vg = vscr.rearrange("(r c) n -> r c n", c=GRID_W)
                for j in range(NJ):
                    for half in range(2):
                        for r in range(4):
                            gp.dma_start(vwin[32 * r:32 * r + 32, 2 * j + half, :],
                                         vg[4 * half + r, COL0[j]:COL0[j] + KB, :]).then_inc(vb_in, 16)

                wait_count(gp, pool_d, l, 4, 4)
                for h in range(8):
                    if h >= 2:
                        wait_count(gp, m_ready, l, NMAPS, MAP0[20 + NT * (h - 2) + NJ])
                    pause(gp)
                    bh = at(bsb, (h % 2) * 1024, NJ, ROWS * KB)
                    gp.dma_start(bh, bias[ds(l * 8 + h, 1)].rearrange("a p j k -> (a p) j k")).then_inc(bias_in[h % 2], 16)
                    gp.wait_ge(bias_in[h % 2], (l * 4 + (h // 2 + 1)) * 16)
                    pause(gp)
                    for j in range(NJ):
                        b3 = bh[:, j, :].rearrange("p (r k) -> p r k", k=KB)
                        op = gp.tensor_tensor(b3, b3, mk[:, j:j + 1, :].broadcast_to([P, ROWS, KB]), ALU.add)
                        op.then_inc(bias_ok, 1)

                wait_count(gp, o_ready, l, NJOBS, NJOBS)
                pause(gp)
                gp.dma_start(sk, subk[ds(l, 1)].rearrange("a p h c -> (a p) h c")).then_inc(subk_in, 16)
                pause(gp)
                with gp.Fori(0, BODIES) as b:
                    for hh in range(2):
                        gp.wait_ge(idx_ready, l * (HEADS * NT + 1) + b * 2 + (hh + 1))
                        for e in range(TOPK):
                            s = e % SLOTS
                            gp.wait_ge(v_done, l * (BODIES * 2 * TOPK) + b * (2 * TOPK) + (hh * TOPK + e + 1))
                            pause(gp)
                            gp.indirect_dma_start(rows[:, s, :], None, experts,
                                                  bass.IndirectOffsetOnAxis(ap=eidx[:, hh, e:e + 1], axis=0)).then_inc(gath[s], 16)
                pause(gp)
                own.tick(gp.memset(st[:, 47:48], 0.0), to=CHAIN_LAYER)

        @block.scalar
        def _(act):
            own = Chain(act, act_own)
            act.wait_ge(ctab, 16)
            act.activation(csil[:], csil[:], ACT.Silu).then_inc(csil_ok, 1)

            with act.Fori(0, DEPTH) as l:
                own.base, own.n = l * CHAIN_LAYER, 0

                def modulation_rows(half):
                    if half:
                        wait_count(act, mod_first, l, 1, 1)
                    pause(act)
                    with act.Fori(0, 2) as it:
                        for b in range(3):
                            c = 4 * b + 3
                            act.wait_ge(w_done[c % RING], l * USES + it * 2 + (4 * half + c // RING + 1))
                            pause(act)
                            act.activation(arena[0:2, ds(it * MOD_STEP + (MOD_ROW + b * 512), 512)],
                                           ps[0:2, 2 * pair(f"ada{6 * half + b}"), :], ACT.Copy).then_inc(free[pair(f"ada{6 * half + b}")], 1)

                def root_of_mean(which):
                    wait_free(act, l, f"rms{which}", 1)
                    act.activation(rstd, rstd, ACT.Sqrt).then_inc(root, 1)

                modulation_rows(0)
                root_of_mean(1)
                wait_count(act, lam_sum, l, 1, 1)
                act.activation(lam[:, 2:4], lam[:, 0:2], ACT.Exp).then_inc(lam_exp, 1)
                modulation_rows(1)

                for i, c in enumerate(range(4)):
                    wait_unit(act, l, f"cb{c}")
                    if i >= 2:
                        wait_count(act, u_ready, l, 4, i - 1)
                    sg = at(T, 640 + 640 * (i % 2), TOK)
                    if i == 0:
                        wait_count(act, h_ready, l, 2 * KD, KD)
                    act.activation(by_half(sg), halves(f"cb{c}"), ACT.Sigmoid).then_inc(free[pair(f"cb{c}")], 1)
                for g in range(4):
                    wait_unit(act, l, f"pl{g}")
                    act.activation(by_half(yT[:, g, :]), halves(f"pl{g}"), ACT.Copy).then_inc(free[pair(f"pl{g}")], 1)
                for t in range(NT):
                    wait_unit(act, l, f"dv{t}")
                    act.activation(dv[:, t, :], banks(f"dv{t}")[0], ACT.Copy).then_inc(free[pair(f"dv{t}")], 1)
                wait_free(act, l, f"dv{NL}", 1)
                pause(act)
                act.dma_start(o_dv[ds(l * P, P)], dv[:, NL, :]).then_inc(state_out, 16)
                for t in range(NL):
                    wait_unit(act, l, f"nv{t}")
                    if t >= 2:
                        wait_count(act, vb_out[t % 2], l * 16, 2, 16)
                    act.activation(vst[:, t % 2, :], banks(f"nv{t}")[0], ACT.Copy).then_inc(free[pair(f"nv{t}")], 1)
                    wait_free(act, l, f"nv{t}", 1)
                    act.dma_start(vscr[t * P:(t + 1) * P, :], vst[:, t % 2, :]).then_inc(vb_out[t % 2], 16)
                wait_unit(act, l, f"nv{NL}")
                act.activation(nv[:, 0, :], banks(f"nv{NL}")[0], ACT.Copy).then_inc(free[pair(f"nv{NL}")], 1)
                wait_free(act, l, f"nv{NL}", 1)
                pause(act)
                act.dma_start(o_nv[ds(l * P, P)], nv[:, 0, :]).then_inc(state_out, 16)

                def qk_square(n):
                    b, t = QK[n]
                    wait_unit(act, l, f"{b}{t}")
                    if n >= 2:
                        wait_count(act, qk_ms, l, 20, n - 1)
                    if n == 0:
                        wait_count(act, u_ready, l, 4, 4)
                    act.activation(at(T, (n % 2) * 512, 512), banks(f"{b}{t}")[0], ACT.Square).then_inc(qk_sq, 1)

                def qk_rt(n):
                    wait_count(act, qk_ms, l, 20, n + 1)
                    act.activation(st[:, (n % 2) * 8:(n % 2) * 8 + 8], st[:, (n % 2) * 8:(n % 2) * 8 + 8], ACT.Sqrt).then_inc(qk_root, 1)

                def qk_out(n):
                    b, t = QK[n]
                    wait_count(act, qk_tr, l, 20, n + 1)
                    src = ps[:, 6 + n % 2, :].rearrange("p (h c) -> p h c", c=P)
                    dst = {"dq": dqT, "dk": dkT, "nq": nqT, "nk": nkT}[b]
                    if b == "nq" and t < NL:
                        for r in range(2):
                            s4 = src[:, :, r * 64:(r + 1) * 64].rearrange("p h (j c) -> p h j c", c=QB)
                            d4 = dst[:, :, 0:LAT].rearrange("p h (j c) -> p h j c", c=P)[:, :, :, (2 * t + r) * QB:(2 * t + r + 1) * QB]
                            op = act.activation(d4, s4, ACT.Copy)
                            if r == 0:
                                own.tick(op)
                    else:
                        op = act.activation(dst[:, :, t * P:(t + 1) * P], src, ACT.Copy)
                    op.then_inc(qk_evac, 1)
                    if b in ("dk", "nk") and t == NL:
                        pause(act)
                        act.dma_start((o_dk if b == "dk" else o_nk)[ds(l * P, P)], at(T, 1024 + (n % 2) * 512, 512)).then_inc(state_out, 16)

                def conv_squares():
                    wait_count(act, cen_ok, l, 1, 1)
                    for c in range(4):
                        own.tick(act.activation(csqv[:, c, 0:LAT], acc[:, c, 0:LAT], ACT.Square))
                        act.activation(csqv[:, c, LAT:TOK], acc[:, c, SPAN - SEQ:SPAN], ACT.Square).then_inc(csq, 1)

                def conv_root():
                    wait_free(act, l, "lnv", 1)
                    act.activation(at(T, 2560, TOK), at(T, 2560, TOK), ACT.Sqrt).then_inc(croot, 1)

                def conv_silu():
                    wait_count(act, cnorm, l, 1, 1)
                    for c in range(4):
                        kw = dict(scale=sm[:, S_LG + c:S_LG + c + 1], bias=sm[:, S_LB + c:S_LB + c + 1])
                        own.link(act.activation(yT[:, 4 + c, 0:LAT], acc[:, c, 0:LAT], ACT.Silu, **kw))
                        op = act.activation(yT[:, 4 + c, LAT:TOK], acc[:, c, SPAN - SEQ:SPAN], ACT.Silu, **kw)
                        if c < 3:
                            own.link(op)
                        else:
                            op.then_inc(y_conv, 1)

                for n in range(len(QK) + 2):
                    if n < len(QK):
                        qk_square(n)
                    if 1 <= n <= len(QK):
                        qk_rt(n - 1)
                    if n >= 2:
                        qk_out(n - 2)
                    if n == LNM_AT:
                        conv_squares()
                    if n == LNV_AT:
                        conv_root()
                    if n == LNV_AT + 3:
                        conv_silu()

                for g in range(4):
                    wait_unit(act, l, f"pw{g}")
                    scl = sm[:, S_PSC + g:S_PSC + g + 1]
                    act.activation(by_half(yT[:, g, :]), halves(f"pw{g}"), ACT.Copy, scale=scl).then_inc(free[pair(f"pw{g}")], 1)
                wait_count(act, state_out, l * 16, 4, 64)

                def map_exp(m):
                    n, i = MAP_JOB[m]
                    width = job_width(JOBS[n][0], JOBS[n][2])
                    o = (n % 2) * 8
                    wait_count(act, m_ready, l, NMAPS, m + 1)
                    act.activation(at(T, (n % 2) * 1280 + i * TOK, width), map_banks(m)[:, 0:width], ACT.Exp,
                                   bias=st[:, o + i:o + i + 1], accum_out=st[:, o + 2 + i:o + 3 + i]).then_inc(exp_done, 1)

                for n, (kind, h, t) in enumerate(JOBS):
                    for m in maps_at(n, 1):
                        map_exp(m)
                    width = job_width(kind, t)
                    wait_count(act, t_ready, l, NJOBS, n + 1)
                    src = ps[:, 4:6, :].rearrange("p b c -> p (b c)")[:, 0:width]
                    act.activation(at(T, 2560, TOK)[:, 0:width], src, ACT.Copy).then_inc(pt_evac, 1)
                    if n:
                        job_out(act, l, n - 1, own, wait_count)
                job_out(act, l, NJOBS - 1, own, wait_count)

                wait_count(act, o_ready, l, NJOBS, NJOBS)
                wait_count(act, o_evac, l, NJOBS, NJOBS)
                for h in range(4):
                    act.activation(at(T, h * TOK, TOK), yT[:, 12 + h, :], ACT.Square).then_inc(dsq, 1)
                for h in range(4):
                    wait_free(act, l, f"dr{h}", 1)
                    act.activation(droots[:, h, :], droots[:, h, :], ACT.Sqrt).then_inc(droot, 1)

                pause(act)
                with act.Fori(0, 4) as dp:
                    for n in range(8):
                        i, dd = n // 2, n % 2
                        c = C_MERGE + 3 * i + dd
                        act.wait_ge(w_done[c % RING], l * USES + dp * 2 + (c // RING + 1))
                        act.wait_ge(br_evac, l * 32 + dp * 8 + (n + 1))
                        pause(act)
                        col = sm[:, ds(dp * 2 + (S_BG + 8 * i + dd), 1)]
                        act.activation(by_half(gt[:, n % 2, :]), halves_at(2 * (n % 2)), ACT.Sigmoid, bias=col).then_inc(gate_evac, 1)

                for d in range(KD):
                    wait_free(act, l, f"o{d}", 1)
                    act.activation(sq2[:, d], x_sb[:, :, d, :], ACT.Square).then_inc(sq_ready, 1)
                root_of_mean(2)

                for n in range(16):
                    if n == 0:
                        wait_count(act, h_ready, l, 2 * KD, 2 * KD)
                    wait_unit(act, l, f"q{n}")
                    if n >= 2:
                        wait_unit(act, l, f"s{n - 2}")
                    act.activation(by_half(qst[:, n % 2, :]), halves(f"q{n}"), ACT.Copy).then_inc(free[pair(f"q{n}")], 1)
                for t in range(NT):
                    wait_unit(act, l, f"hn{t}")
                    act.activation(h_sb[:, t].rearrange("p k c -> p (k c)"), both(f"hn{t}"), ACT.Copy).then_inc(free[pair(f"hn{t}")], 1)

                def numerators(j, par):
                    act.wait_ge(top_ready, j + 1)
                    act.activation(gate[:, par, :], csc[:, par, :], ACT.Exp, bias=st[:, 16 + par:17 + par],
                                   accum_out=st[:, 18 + par:19 + par]).then_inc(gexp, 1)

                numerators(l * (HEADS * NT + 1), 0)
                pause(act)
                with act.Fori(0, NT) as t:
                    with act.Fori(0, HEADS // 2) as q:
                        for hh in range(2):
                            for g in range(GRPS):
                                if g == 2:
                                    numerators(l * (HEADS * NT + 1) + t * HEADS + q * 2 + (hh + 1), (hh + 1) % 2)
                                act.wait_ge(dot, l * (BODIES * 2 * TOPK) + t * (HEADS * TOPK) + q * (2 * TOPK) + (hh * TOPK + (g + 1) * GRP))
                                act.activation(gel[:, hh, g * GRP:(g + 1) * GRP], dots[:, hh, g * GRP:(g + 1) * GRP], ACT.Gelu).then_inc(gelu_ok, 1)
                    act.wait_ge(v_done, l * (BODIES * 2 * TOPK) + t * (HEADS * TOPK) + (HEADS * TOPK + SLOTS))
                    act.wait_ge(y_zero, l * (NT + 1) + t + 1)
                    pause(act)
                    act.activation(h_sb[:, ds(t, 1)].rearrange("p a k c -> p (a k c)"), ps[:, 6:8, :].rearrange("p b c -> p (b c)"), ACT.Copy).then_inc(y_taken, 1)
                    act.wait_ge(y_taken, l * NT + t + 1)
                    pause(act)
                    act.activation(ps[:, 6:8, :].rearrange("p b (s c) -> p (b s) c", c=2 * NKEYS),
                                   scores[:, NT * 16:NT * 16 + 2, :].rearrange("p a c -> p (a c)").unsqueeze(1).broadcast_to([P, 4, 2 * NKEYS]),
                                   ACT.Copy).then_inc(y_zero, 1)
                    pause(act)
                own.tick(act.activation(st[:, 46:47], ident[:, 0:1], ACT.Copy), to=CHAIN_LAYER)

            for t in range(NT):
                act.wait_ge(ready, DEPTH * len(READY) + t + 1)
                b = 2 * (t % 3)
                o = at(arena, t * D, D)
                act.activation(o, ps[:, b:b + 2, :].rearrange("p b c -> p (b c)"), ACT.Copy).then_inc(free[t % 3], 1)
                act.wait_ge(free[t % 3], DEPTH * TURNS + t // 3 + 2)
                act.dma_start(y_sample[t * P:(t + 1) * P, :] if t < NL else y_prompt, o).then_inc(out_done, 16)

        @block.vector
        def _(v):
            own = Chain(v, dve_own)
            for f in free:
                v.sem_inc(f, 1)
            v.sem_inc(br_evac, 2)
            v.sem_inc(v_done, SLOTS)
            v.wait_ge(const_in, 64)
            v.wait_ge(pool_own, 8)
            v.sem_inc(x_ready, 1)

            with v.Fori(0, DEPTH) as l:
                own.base, own.n = l * CHAIN_LAYER, 0
                S = lambda a, n=1: sm[:, a:a + n]

                def rms_inverse(which):
                    u = f"rms{which}"
                    wait_unit(v, l, u)
                    sums = halves(u) if which == 1 else halves_at(6)
                    v.tensor_scalar(by_half(rstd), sums, 1.0 / D, EPS, ALU.mult, ALU.add).then_inc(free[pair(u)], 1)
                    wait_count(v, root, l, 2, which)
                    own.link(v.reciprocal(rstd, rstd))

                def norm_chunk(k):
                    own.tick(v.tensor_tensor(xs[:, :, k, :], x_sb[:, :, k, :], rstd.rearrange("p (t c) -> p t c", c=P), ALU.mult))

                def mod_chunk(which, k):
                    sh = 0 if which == 1 else 24
                    own.tick(v.tensor_scalar(h_sb[:, 0:NL, k, :], xs[:, 0:NL, k, :], amp[:, which - 1, k, 0:1], mod[:, sh + k, 0:1], ALU.mult, ALU.add))
                    v.tensor_scalar(h_sb[:, NL, k, :], xs[:, NL, k, :], amp[:, which - 1, k, 1:2], mod[:, sh + k, 1:2], ALU.mult, ALU.add).then_inc(h_ready, 1)

                def modulation(half):
                    c0, (sc_at, g_at) = 24 * half, ((8, S_N1), (32, S_N2))[half]
                    b = 6 if half == 0 else 2 * pair("mod")
                    src = ps[:, b, 0:48].rearrange("p (c s) -> p c s", s=2)
                    if half == 0:
                        wait_count(v, mod_first, l, 1, 1)
                    else:
                        wait_unit(v, l, "mod")
                    op = v.tensor_tensor(mod[:, c0:c0 + 24, :], src, S(S_BADA + c0, 24).unsqueeze(2).broadcast_to([P, 24, 2]), ALU.add)
                    if half == 0:
                        own.link(op)
                    else:
                        op.then_inc(free[pair("mod")], 1)
                        wait_free(v, l, "mod", 1)
                    own.link(v.scalar_tensor_tensor(amp[:, half], mod[:, sc_at:sc_at + 8, :], 1.0,
                                                    S(g_at, 8).unsqueeze(2).broadcast_to([P, 8, 2]), ALU.add, ALU.mult))

                rms_inverse(1)
                for k in range(KD):
                    norm_chunk(k)
                own.wait()

                wait_count(v, params, l * 16, 3, 48)
                wait_count(v, lam_in, l * 16, 1, 16)
                lr = at(T, 640, 2, 2, 64)
                own.link(v.tensor_tensor(at(T, 896, 2, 64), lr[:, :, 0, :], lr[:, :, 1, :], ALU.mult))
                own.link(v.tensor_reduce(lam[:, 0:2], at(T, 896, 2, 64), AX_X, ALU.add))
                v.sem_inc(lam_sum, 1)
                own.tick(v.tensor_scalar(rg[:, 0:64], rg[:, 0:64], 0.125, None, ALU.mult))
                own.tick(v.tensor_scalar(rg[:, 128:192], rg[:, 128:192], 0.125, None, ALU.mult))
                own.link(v.tensor_tensor(lam[:, 5:6], S(S_SUB), cl[:, 1:2], ALU.mult))
                wait_count(v, lam_exp, l, 1, 1)
                own.link(v.tensor_tensor(lam[:, 4:5], lam[:, 3:4], lam[:, 2:3], ALU.subtract))
                own.tick(v.tensor_tensor(lam[:, 4:5], lam[:, 4:5], cl[:, 0:1], ALU.subtract))

                modulation(0)
                for k in range(KD):
                    mod_chunk(1, k)

                wait_count(v, conv_pool, l, 1, 1)
                for i, c in enumerate(range(4)):
                    wait_unit(v, l, f"ca{c}")
                    wait_free(v, l, f"cb{c}", 1)
                    a5 = halves(f"ca{c}")
                    g5 = by_half(at(T, 640 + 640 * (i % 2), TOK))
                    own.tick(v.tensor_tensor(by_half(U[:, c, LAT0:LAT0 + LAT]), a5[:, 0:NL], g5[:, 0:NL], ALU.mult))
                    v.tensor_tensor(by_half(U[:, c, CTX0:CTX0 + SEQ]), a5[:, NL:NT], g5[:, NL:NT], ALU.mult).then_inc(free[pair(f"ca{c}")], 1)
                    wait_free(v, l, f"ca{c}", 1)
                    own.wait()
                    v.sem_inc(u_ready, 1)
                modulation(1)
                for k in range(CONV_W):
                    for c in range(4):
                        if k:
                            v.wait_ge(dve_own, own.base + own.n - 3)
                            col = S_CW + c * CONV_W + k
                            op = v.scalar_tensor_tensor(acc[:, c, :], U[:, c, 1 + k:1 + k + SPAN], S(col), acc[:, c, :], ALU.mult, ALU.add)
                        else:
                            op = v.tensor_scalar(acc[:, c, :], U[:, c, 1:1 + SPAN], S(S_CW + c * CONV_W), S(S_CB + c), ALU.mult, ALU.add)
                        own.tick(op)
                own.wait()
                v.sem_inc(conv_done, 1)

                def qk_mean(n):
                    b, t = QK[n]
                    o = (n % 2) * 8
                    wait_count(v, qk_sq, l, 20, n + 1)
                    own.link(v.tensor_reduce(st[:, o:o + 8], at(T, (n % 2) * 512, 8, 64), AX_X, ALU.add))
                    v.tensor_scalar(st[:, o:o + 8], st[:, o:o + 8], 1.0 / 64, EPS, ALU.mult, ALU.add).then_inc(qk_ms, 1)

                def qk_norm(n):
                    b, t = QK[n]
                    o = (n % 2) * 8
                    qn = at(T, 1024 + (n % 2) * 512, 8, 64)
                    wait_count(v, qk_root, l, 20, n + 1)
                    own.link(v.reciprocal(st[:, 16 + o:24 + o], st[:, o:o + 8]))
                    if n >= 2:
                        wait_count(v, qk_tr, l, 20, n - 1)
                    if n == 11:
                        wait_count(v, state_out, l * 16, 4, 48)
                    unit = f"{b}{t}"
                    src = banks(unit)[0].rearrange("p (h c) -> p h c", c=64)
                    v.tensor_tensor(qn, src, st[:, 16 + o:24 + o].unsqueeze(2).broadcast_to([P, 8, 64]), ALU.mult).then_inc(free[pair(unit)], 1)
                    wait_free(v, l, unit, 1)
                    g0 = {"nq": 0, "nk": 64, "dq": 128, "dk": 192}[b]
                    gain = rg[:, g0:g0 + 64].unsqueeze(1).broadcast_to([P, 8, 64])
                    if b[0] == "n" or t == NL:
                        v.tensor_tensor(qn, qn, gain, ALU.mult).then_inc(qk_fin, 1)
                        return
                    own.link(v.tensor_tensor(qn, qn, gain, ALU.mult))
                    rot = at(T, 2048, 8, 64)
                    q5 = qn.rearrange("p h (a s f) -> p h a s f", a=2, s=2)
                    r5 = rot.rearrange("p h (a s f) -> p h a s f", a=2, s=2)
                    s4 = rp[:, t, 1, :].rearrange("p (a s f) -> p a s f", a=2, s=2)
                    for s in range(2):
                        for a in range(2):
                            own.tick(v.tensor_tensor(r5[:, :, a, s, :], q5[:, :, a, 1 - s, :], s4[:, a, s, :].unsqueeze(1).broadcast_to([P, 8, 16]), ALU.mult))
                    own.wait()
                    own.link(v.tensor_tensor(qn, qn, rp[:, t, 0, :].unsqueeze(1).broadcast_to([P, 8, 64]), ALU.mult))
                    v.tensor_tensor(qn, qn, rot, ALU.add).then_inc(qk_fin, 1)

                def seqs(ap3):
                    return ((ap3[:, :, 0:LAT], 0, LAT), (ap3[:, :, SPAN - SEQ:SPAN], LAT, TOK))

                rs = at(T, 2560, TOK)

                def conv_centre():
                    wait_unit(v, l, "lnm")
                    for (a3, s, e), b in zip(seqs(acc), banks("lnm")):
                        n = e - s
                        op = v.scalar_tensor_tensor(a3, b.unsqueeze(1).broadcast_to([P, 4, n]), -1.0 / BW, a3, ALU.mult, ALU.add)
                        if s == 0:
                            own.link(op)
                    op.then_inc(free[pair("lnm")], 1)
                    wait_free(v, l, "lnm", 1)
                    v.sem_inc(cen_ok, 1)

                def conv_variance():
                    wait_unit(v, l, "lnv")
                    v.tensor_scalar(by_half(rs), halves("lnv"), 1.0 / BW, EPS, ALU.mult, ALU.add).then_inc(free[pair("lnv")], 1)

                def conv_norm():
                    wait_count(v, croot, l, 1, 1)
                    own.link(v.reciprocal(rs, rs))
                    for a3, s, e in seqs(acc):
                        op = v.tensor_tensor(a3, a3, rs[:, s:e].unsqueeze(1).broadcast_to([P, 4, e - s]), ALU.mult)
                        if s == 0:
                            own.tick(op)
                    op.then_inc(cnorm, 1)

                for n in range(len(QK) + 1):
                    if n < len(QK):
                        qk_mean(n)
                    if n >= 1:
                        qk_norm(n - 1)
                    if n == LNM_AT:
                        conv_centre()
                    if n == LNV_AT:
                        conv_variance()
                    if n == LNV_AT + 1:
                        conv_norm()

                def map_max(m):
                    n, i = MAP_JOB[m]
                    kind, h, t = JOBS[n]
                    o = (n % 2) * 8
                    wait_count(v, s_ready, l, NMAPS, m + 1)
                    src = map_banks(m)[:, 0:job_width(kind, t)]
                    if kind == "nat" and t < NL:
                        wait_count(v, bias_ok, l, 32, NJ * h + t + 1)
                        loc = src[:, 0:ROWS * KB]
                        own.link(v.tensor_tensor(loc, loc, at(bsb, (h % 2) * 1024, NJ, ROWS * KB)[:, t, :], ALU.add))
                    own.link(v.tensor_reduce(st[:, o + 4 + i:o + 5 + i], src, AX_X, ALU.max))
                    v.tensor_scalar(st[:, o + i:o + i + 1], st[:, o + 4 + i:o + 5 + i], -1.0, None, ALU.mult).then_inc(m_ready, 1)

                def job_probs(n):
                    kind, h, t = JOBS[n]
                    width = job_width(kind, t)
                    o, maps = (n % 2) * 8, MAPS[n]
                    wait_count(v, exp_done, l, NMAPS, MAP0[n] + maps)
                    P0 = at(T, (n % 2) * 1280, width)
                    P1 = at(T, (n % 2) * 1280 + TOK, width)
                    own.link(v.reciprocal(st[:, o + 6:o + 6 + maps], st[:, o + 2:o + 2 + maps]))
                    op = v.tensor_scalar(P0, P0, st[:, o + 6:o + 7], None, ALU.mult)
                    if kind == "diff":
                        own.tick(op)
                        own.link(v.tensor_tensor(st[:, o + 7:o + 8], st[:, o + 7:o + 8], lam[:, 4:5], ALU.mult))
                        op = v.scalar_tensor_tensor(P0, P1, st[:, o + 7:o + 8], P0, ALU.mult, ALU.add)
                    op.then_inc(pd_ready, 1)

                for n in range(NJOBS):
                    for m in maps_at(n, 1):
                        map_max(m)
                    job_probs(n)

                for h in range(4):
                    wait_unit(v, l, f"dr{h}")
                    v.tensor_scalar(by_half(droots[:, h, :]), halves(f"dr{h}"), 1.0 / P, EPS, ALU.mult, ALU.add).then_inc(free[pair(f"dr{h}")], 1)
                for h in range(4):
                    r = droots[:, h, :]
                    wait_count(v, droot, l, 4, h + 1)
                    own.link(v.reciprocal(r, r))
                    v.scalar_tensor_tensor(yT[:, 12 + h, :], yT[:, 12 + h, :], lam[:, 5:6], r, ALU.mult, ALU.mult).then_inc(y_diff, 1)

                MERGE = 48
                m0, outer = own.n, own.base
                pause(v)
                with v.Fori(0, 4) as dp:
                    own.base, own.n = outer + m0 + dp * MERGE, 0
                    for n in range(8):
                        i, dd = n // 2, n % 2
                        v.wait_ge(gate_evac, l * 32 + dp * 8 + (n + 1))
                        if dd:
                            c = C_MERGE + 3 * i + 2
                            v.wait_ge(w_done[c % RING], l * USES + dp * 2 + (c // RING + 1))
                        else:
                            v.wait_ge(br_ready, l * 16 + dp * 4 + (i + 1))
                        m = merged[:, ds(dp * 2 + dd, 1), :].rearrange("p a c -> p (a c)")
                        dst = m if i == 0 else prod[:, n % 2, :]
                        v.tensor_tensor(by_half(dst), halves_at(4 + 2 * (n % 2)), by_half(gt[:, n % 2, :]), ALU.mult).then_inc(br_evac, 1)
                        if i:
                            v.wait_ge(br_evac, l * 32 + dp * 8 + (n + 3))
                            if i > 1:
                                own.wait()
                            op = v.tensor_tensor(m, m, prod[:, n % 2, :], ALU.add)
                            own.tick(op, to=MERGE if n == 7 else None)
                    own.wait()
                    v.sem_inc(merged_ok, 1)
                own.base, own.n = outer, m0 + 4 * MERGE

                for d in range(KD):
                    u = f"o{d}"
                    wait_unit(v, l, u)
                    o5, x5 = halves(u), split_half(x_sb[:, :, d, :])
                    for s in range(2):
                        own.tick(v.scalar_tensor_tensor(x5[:, 0:NL, s], o5[:, 0:NL, s], mod[:, 16 + d, 0:1], x5[:, 0:NL, s], ALU.mult, ALU.add))
                    v.scalar_tensor_tensor(x5[:, NL:NT], o5[:, NL:NT], mod[:, 16 + d, 1:2], x5[:, NL:NT], ALU.mult, ALU.add).then_inc(free[pair(u)], 1)
                wait_free(v, l, f"o{KD - 1}", 1)
                own.wait()
                rms_inverse(2)
                norm_chunk(0)
                for k in range(KD):
                    own.wait()
                    if k + 1 < KD:
                        norm_chunk(k + 1)
                    mod_chunk(2, k)

                def route(j, par):
                    own.link(v.tensor_copy(sc, scores[:, ds(j * 2, 2), :]))
                    for p in range(2):
                        pause(v)
                        own.tick(v.max(top[:, p, 0:8], sc[:, p, :]))
                    own.wait()
                    for p in range(2):
                        pause(v)
                        own.tick(v.max_index(topi[:, p, 0:8], top[:, p, 0:8], sc[:, p, :]))
                        pause(v)
                        own.tick(v.match_replace(screp[:, p, :], top[:, p, 0:8], sc[:, p, :], LOWEST))
                    own.wait()
                    for p in range(2):
                        pause(v)
                        own.tick(v.max(top[:, p, 8:16], screp[:, p, :]))
                    own.wait()
                    for p in range(2):
                        pause(v)
                        own.tick(v.max_index(topi[:, p, 8:16], top[:, p, 8:16], screp[:, p, :]))
                    yield
                    own.tick(v.tensor_tensor(cand, top[:, 0, :].unsqueeze(2).broadcast_to([P, TOPK, TOPK]),
                                             top[:, 1, :].unsqueeze(1).broadcast_to([P, TOPK, TOPK]), ALU.add))
                    own.wait()
                    own.tick(v.tensor_copy(topf, topi[:]))
                    flat = cand.rearrange("p a b -> p (a b)")
                    pause(v)
                    own.link(v.max(csc[:, par, 0:8], flat))
                    pause(v)
                    own.tick(v.max_index(ci[:, 0, 0:8], csc[:, par, 0:8], flat))
                    pause(v)
                    own.link(v.match_replace(crep, csc[:, par, 0:8], flat, LOWEST))
                    pause(v)
                    own.link(v.max(csc[:, par, 8:16], crep))
                    v.tensor_scalar(st[:, 16 + par:17 + par], csc[:, par, 0:1], -1.0, None, ALU.mult).then_inc(top_ready, 1)
                    pause(v)
                    own.link(v.max_index(ci[:, 0, 8:16], csc[:, par, 8:16], crep))
                    yield
                    own.tick(v.tensor_scalar(ci[:, 1, :], ci[:, 0, :], 4, None, ALU.logical_shift_right))
                    own.link(v.tensor_scalar(ci[:, 2, :], ci[:, 0, :], 15, None, ALU.bitwise_and))
                    own.link(v.tensor_copy(abf, ci[:, 1:3, :]))
                    for p in range(2):
                        own.tick(v.tensor_tensor(hot[:, p], abf[:, p, :].unsqueeze(2).broadcast_to([P, TOPK, TOPK]),
                                                 iota.unsqueeze(1).broadcast_to([P, TOPK, TOPK]), ALU.is_equal))
                    own.wait()
                    for p in range(2):
                        own.tick(v.tensor_tensor(hot[:, p], hot[:, p], topf[:, p, :].unsqueeze(1).broadcast_to([P, TOPK, TOPK]), ALU.mult))
                    own.wait()
                    own.link(v.tensor_reduce(sel, hot, AX_X, ALU.add))
                    own.link(v.scalar_tensor_tensor(ef, sel[:, 0, :], float(NKEYS), sel[:, 1, :], ALU.mult, ALU.add))
                    v.tensor_scalar(eidx[:, par, :], ef, cl[:, 2:3], None, ALU.add).then_inc(idx_ready, 1)

                sc4 = scores[:, 0:NT * 16, :].rearrange("p (t n) c -> p t n c", t=NT)
                wait_count(v, h_ready, l, 2 * KD, 2 * KD)
                own.tick(v.memset(scores[:, NT * 16:NT * 16 + 2, :], 0.0))
                own.tick(v.memset(ps[:, 6:8, :], 0.0))
                own.tick(v.tensor_copy(iota, iota_i[:]))
                first = None
                for n in range(16):
                    u = f"s{n}"
                    wait_unit(v, l, u)
                    b0, b1 = banks(u)
                    own.tick(v.tensor_copy(sc4[:, 0:NL, n, :], tile4(b0)))
                    v.tensor_copy(sc4[:, NL, n, :], b1).then_inc(free[pair(u)], 1)
                    if n == 1:
                        wait_free(v, l, "s0", 1)
                        wait_free(v, l, "s1", 1)
                        own.wait()
                        first = route(0, 0)
                    if first:
                        next(first, None)
                wait_free(v, l, "s15", 1)
                wait_free(v, l, "s14", 1)
                own.wait()
                v.sem_inc(y_zero, 1)

                def process(hj, gj, hh, steps):
                    for g in range(GRPS):
                        for e in range(GRP):
                            x = g * GRP + e
                            s = x % SLOTS
                            v.wait_ge(gath[s], (gj * 2 + (x // SLOTS + 1)) * 16)
                            pause(v)
                            v.tensor_tensor_reduce(rows[:, s, 0:D], rows[:, s, 0:D], hcur, 1.0, 0.0,
                                                   ALU.mult, ALU.add, dots[:, hh, x:x + 1]).then_inc(dot, 1)
                        if g == 0:
                            v.wait_ge(gexp, hj + 1)
                            own.link(v.reciprocal(st[:, 20 + hh:21 + hh], st[:, 18 + hh:19 + hh]))
                            own.link(v.tensor_scalar(gate[:, hh, :], gate[:, hh, :], st[:, 20 + hh:21 + hh], None, ALU.mult))
                        next(steps, None)
                        v.wait_ge(gelu_ok, gj * GRPS + (g + 1))
                        cols = slice(g * GRP, (g + 1) * GRP)
                        own.link(v.tensor_tensor(wgt[:, hh, cols], gel[:, hh, cols], gate[:, hh, cols], ALU.mult))
                        v.tensor_tensor(dg[:, g % 2], ident[:].unsqueeze(1).broadcast_to([P, GRP, P]),
                                        wgt[:, hh, cols].unsqueeze(2).broadcast_to([P, GRP, P]), ALU.mult).then_inc(dg_ready, 1)

                hcur = at(bsb, 1024, D)
                p0, outer = own.n, own.base
                pause(v)
                with v.Fori(0, NT) as t:
                    own.base, own.n = outer + p0 + t * CHAIN_TILE, 0
                    wait_free(v, l, f"hn{NT - 1}", 1)
                    wait_free(v, l, f"hn{NT - 2}", 1)
                    wait_free(v, l, f"hn{NT - 3}", 1)
                    pause(v)
                    own.link(v.tensor_copy(hcur, h_sb[:, ds(t, 1)].rearrange("p a k c -> p (a k c)")))
                    pause(v)
                    with v.Fori(0, HEADS // 2) as q:
                        own.base, own.n = outer + (p0 + 1) + t * CHAIN_TILE + q * CHAIN_BODY, 0
                        for hh in range(2):
                            steps = route(t * HEADS + q * 2 + (hh + 1), (hh + 1) % 2)
                            before = l * (HEADS * NT) + t * HEADS + q * 2 + hh
                            process(l * (HEADS * NT + 1) + t * HEADS + q * 2 + hh, before, hh, steps)
                        own.link(v.tensor_copy(st[:, 22:23], st[:, 16:17]), to=CHAIN_BODY)
                own.base, own.n = outer, p0 + NT * CHAIN_TILE

                for t in range(NT):
                    u = f"yn{t}"
                    wait_unit(v, l, u)
                    src = both(u).rearrange("p (k c) -> p k c", c=P)
                    s = 0 if t < NL else 1
                    for k in range(KD):
                        op = v.scalar_tensor_tensor(x_sb[:, t, k, :], src[:, k, :], mod[:, 40 + k, s:s + 1], x_sb[:, t, k, :], ALU.mult, ALU.add)
                        if k < KD - 1:
                            own.tick(op)
                    op.then_inc(free[pair(u)], 1)
                for t in range(2, NT):
                    wait_free(v, l, f"yn{t}", 1)
                own.link(v.tensor_copy(st[:, 23:24], st[:, 16:17]), to=CHAIN_LAYER)
                v.sem_inc(x_ready, 1)

        @block.tensor
        def _(pe):
            pe.wait_ge(csil_ok, 1)
            pe.wait_ge(pool_own, 8)

            def project(u, l, src, c, h_at=None):
                wait_chunk(pe, l, c)
                wait_free(pe, l, u)
                for k in range(KD):
                    if h_at is not None:
                        wait_count(pe, h_ready, l, 2 * KD, h_at + k + 1)
                    for s in range(2):
                        mm = pe.matmul(ps[:, 2 * pair(u) + s, 0:TOK // 2], wring[:, c % RING, k * P:(k + 1) * P],
                                       src(k)[:, :, s, :], start=(k == 0), stop=(k == KD - 1))
                mm.then_inc(w_done[c % RING], 1)

            def h_in(k):
                return split_half(h_sb[:, :, k, :])

            def half_sums(u, parts):
                for i, x in enumerate(parts):
                    for s in range(2):
                        mm = pe.matmul(ps[:, 2 * pair(u) + s, 0:TOK // 2], ones[:], x[:, :, s, :],
                                       start=(i == 0), stop=(i == len(parts) - 1))
                mm.then_inc(ready, 1)

            def ones_sum(u, l, parts0, parts1):
                b0, b1 = banks(u)
                for i, x in enumerate(parts0):
                    pe.matmul(b0, ones[:], x, start=(i == 0), stop=(i == len(parts0) - 1))
                for i, x in enumerate(parts1):
                    mm = pe.matmul(b1, ones[:], x, start=(i == 0), stop=(i == len(parts1) - 1))
                mm.then_inc(ready, 1)

            def token_units(name, l, c0):
                for t in range(NT):
                    u = f"{name}{t}"
                    wait_free(pe, l, u)
                    for q in range(4):
                        if t == 0:
                            wait_chunk(pe, l, c0 + q)
                        for kk in range(2):
                            k = 2 * q + kk
                            mm = pe.matmul(banks(u)[0], h_sb[:, t, k, :], wring[:, (c0 + q) % RING, kk * 512:(kk + 1) * 512],
                                           start=(k == 0), stop=(k == KD - 1))
                        if t == NT - 1:
                            mm.then_inc(w_done[(c0 + q) % RING], 1)
                    if t < NT - 1:
                        mm.then_inc(ready, 1)
                    yield u

            with pe.Fori(0, DEPTH) as l:
                def modulation_products(half):
                    pause(pe)
                    with pe.Fori(0, 2) as it:
                        for b in range(3):
                            n = UNIT[f"ada{6 * half + b}"]
                            pe.wait_ge(free[n % 3], l * TURNS + it + (n // 3 + 1))
                            for q in range(4):
                                c = 4 * b + q
                                wait_chunk(pe, l, c, it * 2 + 4 * half)
                                for kk in range(2):
                                    k = 2 * q + kk
                                    mm = pe.matmul(ps[0:2, 2 * (n % 3), :], csil[:, k, :], wring[:, c % RING, kk * 512:(kk + 1) * 512],
                                                   start=(k == 0), stop=(k == KD - 1))
                                mm.then_inc(w_done[c % RING], 1)

                def modulation_columns(half, bank):
                    for b in range(3):
                        wait_free(pe, l, f"ada{6 * half + 3 + b}", 1)
                    for c in range(24):
                        at0 = MOD_ROW + c // 12 * MOD_STEP + c % 12 * P
                        mm = pe.matmul(ps[:, bank, 2 * c:2 * c + 2], arena[0:2, at0:at0 + P], ident[0:2, 0:2],
                                       start=True, stop=True)
                    return mm

                modulation_products(0)
                wait_free(pe, l, "rms1")
                wait_count(pe, sq_ready, l, NT + KD, NT)
                half_sums("rms1", [split_half(sq[:, :, k, :]) for k in range(KD)])
                modulation_columns(0, 6).then_inc(mod_first, 1)
                modulation_products(1)
                for c in range(4):
                    project(f"cb{c}", l, h_in, CHUNK_OF[f"cb{c}"], 0 if c == 0 else None)
                    project(f"ca{c}", l, h_in, CHUNK_OF[f"ca{c}"])
                wait_free(pe, l, "mod")
                modulation_columns(1, 2 * pair("mod")).then_inc(ready, 1)
                for g in range(4):
                    project(f"pl{g}", l, h_in, CHUNK_OF[f"pl{g}"])
                for i, name in enumerate(("dv", "nv")):
                    for _u in token_units(name, l, C_V + 4 * i):
                        pass

                def qk_units():
                    for i, b in enumerate(("dq", "dk", "nq", "nk")):
                        yield from token_units(b, l, C_QK + 4 * i)

                def qk_transpose(n):
                    wait_count(pe, qk_fin, l, 20, n + 1)
                    if n >= 2:
                        wait_count(pe, qk_evac, l, 20, n - 1)
                    qn = at(T, 1024 + (n % 2) * 512, 4, P)
                    for h in range(4):
                        mm = pe.transpose(ps[:, 6 + n % 2, h * P:(h + 1) * P], qn[:, h, :], ident[:])
                    mm.then_inc(qk_tr, 1)

                def conv_sums():
                    wait_free(pe, l, "lnm")
                    wait_count(pe, conv_done, l, 1, 1)
                    ones_sum("lnm", l, [acc[:, c, 0:LAT] for c in range(4)], [acc[:, c, SPAN - SEQ:SPAN] for c in range(4)])

                def conv_square_sums():
                    wait_free(pe, l, "lnv")
                    wait_count(pe, csq, l, 4, 4)
                    half_sums("lnv", [by_half(csqv[:, c, :]) for c in range(4)])

                for n, _u in enumerate(qk_units()):
                    if n >= 2:
                        qk_transpose(n - 2)
                    if n == LNM_AT:
                        conv_sums()
                    if n == LNV_AT:
                        conv_square_sums()
                for n in range(len(QK) - 2, len(QK)):
                    qk_transpose(n)

                wait_count(pe, pool_in, l * 16, 1, 16)
                for g in range(4):
                    u = f"pw{g}"
                    wait_free(pe, l, u)
                    wait_count(pe, pool_d, l, 4, g + 1)
                    for s in range(2):
                        mm = pe.matmul(ps[:, 2 * pair(u) + s, 0:TOK // 2], pw_sb[:, g, :], by_half(yT[:, g, :])[:, :, s, :],
                                       start=True, stop=True)
                    mm.then_inc(ready, 1)

                def keys(kind, h, i, t):
                    if kind == "diff":
                        lo, qT, kT, c = 64 * i, dqT, dkT, h
                    else:
                        lo, qT, kT, c = 64 * (h % 2), nqT, nkT, h // 2
                    q = qT[lo:lo + 64, c, t * P:(t + 1) * P]
                    k = kT[lo:lo + 64, c, :]
                    if t == NL:
                        return q, [(k[:, LAT:TOK], SEQ)]
                    if kind == "diff":
                        return q, [(k[:, 0:LAT], LAT), (k[:, TOK:TOK + PAST], PAST)]
                    win = k[:, 0:LAT].rearrange("p (r c) -> p r c", c=GRID_W)[:, :, COL0[t]:COL0[t] + KB]
                    return q, [(win, ROWS * KB), (k[:, TOK:TOK + PAST], PAST)]

                def values(kind, h, t):
                    if kind == "diff":
                        c = slice(h * P, (h + 1) * P)
                        return [dv[:, NL, c]] if t == NL else [dv[:, i, c] for i in (0, 1, 2, 3, 5)]
                    c = slice((h // 2) * P, (h // 2 + 1) * P)
                    return [nv[:, 0, c]] if t == NL else [vwin[:, 2 * t, c], vwin[:, 2 * t + 1, c], nv[:, 1, c]]

                def map_scores(m):
                    n, i = MAP_JOB[m]
                    kind, h, t = JOBS[n]
                    if m >= 2:
                        wait_count(pe, exp_done, l, NMAPS, m - 1)
                    q, ks = keys(kind, h, i, t)
                    start = 0
                    for k, width in ks:
                        b = 2 * (m % 2) + start // 512
                        mm = pe.matmul(ps[:, b, start % 512:start % 512 + width], q, k, start=True, stop=True, skip_group_check=True)
                        start += width
                    mm.then_inc(s_ready, 1)

                for u in ("pw1", "pw2", "pw3"):
                    wait_free(pe, l, u, 1)
                wait_count(pe, qk_evac, l, 20, 20)
                wait_count(pe, ctx_in, l * 16, 4, 64)
                wait_count(pe, y_conv, l, 1, 1)

                def job_values(n):
                    kind, h, t = JOBS[n]
                    vs = values(kind, h, t)
                    if kind == "nat" and h == 0 and t == 0:
                        wait_count(pe, vb_in, l * 16, 32, 512)
                    wait_count(pe, pt_evac, l, NJOBS, n + 1)
                    if n >= 2:
                        wait_count(pe, o_evac, l, NJOBS, n - 1)
                    pt = at(T, 2560, 5, P)
                    for i, x in enumerate(vs):
                        mm = pe.matmul(ps[:, 6 + n % 2, 0:P], x, pt[:, i, :], start=(i == 0), stop=(i == len(vs) - 1))
                    mm.then_inc(o_ready, 1)

                for n, (kind, h, t) in enumerate(JOBS):
                    for m in maps_at(n, 2):
                        map_scores(m)
                    if n:
                        job_values(n - 1)
                    wait_count(pe, pd_ready, l, NJOBS, n + 1)
                    Pn = at(T, (n % 2) * 1280, TOK)
                    for i in range(job_width(kind, t) // P):
                        mm = pe.transpose(ps[:, 4 + i // 4, (i % 4) * P:(i % 4 + 1) * P], Pn[:, i * P:(i + 1) * P], ident[:])
                    mm.then_inc(t_ready, 1)
                job_values(NJOBS - 1)

                for h in range(4):
                    u = f"dr{h}"
                    wait_free(pe, l, u)
                    wait_count(pe, dsq, l, 4, h + 1)
                    half_sums(u, [by_half(at(T, h * TOK, TOK))])

                for h in range(1, 4):
                    wait_free(pe, l, f"dr{h}", 1)
                pause(pe)
                with pe.Fori(0, 4) as dp:
                    for n in range(8):
                        i, dd = n // 2, n % 2
                        if n == 6:
                            wait_count(pe, y_diff, l, 4, 4)
                        c = C_MERGE + 3 * i + dd
                        wait_chunk(pe, l, c, dp * 2)
                        pe.wait_ge(br_evac, l * 32 + dp * 8 + (n + 1))
                        g = 2 * (n % 2)
                        for k in range(KD):
                            wk = wring[:, c % RING, k * P:(k + 1) * P]
                            for s in range(2):
                                mm = pe.matmul(ps[:, g + s, 0:TOK // 2], wk, h_in(k)[:, :, s, :], start=(k == 0), stop=(k == KD - 1))
                        mm.then_inc(w_done[c % RING], 1)
                        c = C_MERGE + 3 * i + 2
                        wait_chunk(pe, l, c, dp * 2)
                        for k in range(4):
                            wk = wring[:, c % RING, (dd * 4 + k) * P:(dd * 4 + k + 1) * P]
                            for s in range(2):
                                mm = pe.matmul(ps[:, 4 + g + s, 0:TOK // 2], wk, by_half(yT[:, 4 * i + k, :])[:, :, s, :], start=(k == 0), stop=(k == 3))
                        mm.then_inc(w_done[c % RING] if dd else br_ready, 1)

                wait_count(pe, merged_ok, l, 4, 4)
                def square_sums(d):
                    wait_count(pe, sq_ready, l, NT + KD, NT + d + 1)
                    for s in range(2):
                        mm = pe.matmul(ps[:, 6 + s, 0:TOK // 2], ones[:], split_half(sq2[:, d])[:, :, s, :],
                                       start=(d == 0), stop=(d == KD - 1), skip_group_check=True)
                    if d == KD - 1:
                        mm.then_inc(ready, 1)

                for d in range(KD):
                    project(f"o{d}", l, lambda k: by_half(merged[:, k, :]), C_OUT + d)
                    if d >= 2:
                        square_sums(d - 2)
                square_sums(KD - 2)
                square_sums(KD - 1)
                wait_free(pe, l, "rms2")


                def peer_scores(n):
                    u = f"s{n}"
                    if n == 0:
                        wait_count(pe, subk_in, l * 16, 1, 16)
                    wait_free(pe, l, f"q{n}", 1)
                    wait_free(pe, l, u)
                    b0, b1 = banks(u)
                    for t in range(NT):
                        o = b0[:, t * P:(t + 1) * P] if t < NL else b1
                        mm = pe.matmul(o, qst[:, n % 2, t * P:(t + 1) * P], sk[:, n, :], start=True, stop=True)
                    mm.then_inc(ready, 1)

                for n in range(16):
                    project(f"q{n}", l, h_in, C_QUERY + n, KD if n == 0 else None)
                    if n:
                        peer_scores(n - 1)
                peer_scores(15)

                def turn_tiles(name):
                    for t in range(NT):
                        u = f"{name}{t}"
                        wait_free(pe, l, u)
                        for k in range(KD):
                            mm = pe.transpose(both(u)[:, k * P:(k + 1) * P], h_sb[:, t, k, :], ident[:])
                        mm.then_inc(ready, 1)

                turn_tiles("hn")

                pause(pe)
                with pe.Fori(0, NT) as t:
                    pe.wait_ge(y_zero, l * (NT + 1) + t + 1)
                    pause(pe)
                    with pe.Fori(0, HEADS // 2) as q:
                        for n in range(2 * GRPS):
                            pe.wait_ge(dg_ready, l * (BODIES * 2 * GRPS) + t * (HEADS * GRPS) + q * (2 * GRPS) + (n + 1))
                            for e in range(GRP):
                                s = (n * GRP + e) % SLOTS
                                for c in range(2):
                                    mm = pe.matmul(ps[:, 6 + c, :], dg[:, n % 2, e, :], rows[:, s, D + c * 512:D + (c + 1) * 512],
                                                   start=False, stop=False, skip_group_check=True)
                                mm.then_inc(v_done, 1)
                pe.wait_ge(y_zero, l * (NT + 1) + NT + 1)
                turn_tiles("yn")

            pe.wait_ge(x_ready, DEPTH + 1)
            for t in range(NT):
                pe.wait_ge(free[t % 3], DEPTH * TURNS + t // 3 + 1)
                b = 2 * (t % 3)
                for k in range(KD):
                    mm = pe.transpose(ps[:, b + k // 4, (k % 4) * P:(k % 4 + 1) * P], x_sb[:, t, k, :], ident[:])
                mm.then_inc(ready, 1)


def _col_chunks(m):
    n = m.shape[1] // P
    return m.reshape(KD, P, n, P).transpose(2, 1, 0, 3).reshape(n, P, 1024)


def _row_chunks(m):
    n = m.shape[1] // 512
    return m.reshape(4, 2, P, n, 512).transpose(3, 0, 2, 1, 4).reshape(4 * n, P, 1024)


def _chans(v):
    return v.reshape(-1, P).T


def kernel(**inputs):
    import concourse.bacc as bacc
    from concourse.bass_utils import run_bass_kernel_spmd

    a = {k: np.asarray(x) for k, x in inputs.items()}
    order = (0, 2, 1, 3)
    stream, small, rowg, lamrow = [], [], [], []
    for l in range(DEPTH):
        wi = a["w_in"][l]
        parts = [_row_chunks(a["w_ada"][l])]
        ca, cb = _col_chunks(wi[:, 2048:2560]), _col_chunks(wi[:, 2560:3072])
        for c in range(4):
            parts += [cb[c:c + 1], ca[c:c + 1]]
        parts.append(_col_chunks(wi[:, 0:512]))
        for s in (4096, 1536, 3072, 3584, 512, 1024):
            parts.append(_row_chunks(wi[:, s:s + 512]))
        wg = _col_chunks(a["w_gate"][l])
        wb = a["w_branch"][l].reshape(4, 4, P, 4, 2, P)
        for dp in range(4):
            for i in order:
                parts += [wg[8 * i + 2 * dp:8 * i + 2 * dp + 2], wb[i, :, :, dp].transpose(1, 2, 0, 3).reshape(1, P, 1024)]
        parts += [_col_chunks(a["w_out"][l]), _col_chunks(a["peer_w_query"][l])]
        stream.append(np.concatenate(parts))
        small.append(np.concatenate([
            _chans(a["b_ada"][l]), _chans(a["norm1_g"][l]), _chans(a["norm2_g"][l]), _chans(a["pool_scale"][l]),
            a["conv_w"][l].reshape(CONV_W, 4, P).transpose(2, 1, 0).reshape(P, 4 * CONV_W),
            _chans(a["conv_b"][l]), _chans(a["conv_ln_g"][l]), _chans(a["conv_ln_b"][l]), _chans(a["diff_subln_g"][l]),
            _chans(a["b_gate"][l].reshape(4, D)[list(order)]),
        ], axis=1))
        rowg.append(np.broadcast_to(np.concatenate([a[n][l] for n in ("nat_q_g", "nat_k_g", "diff_q_g", "diff_k_g")]), (P, 256)))
        lamrow.append(np.broadcast_to(a["diff_lambda_p"][l].reshape(256), (P, 256)))

    lam_init = [0.8 - 0.6 * float(np.exp(-0.3 * l)) for l in range(DEPTH)]
    clay = np.zeros((DEPTH, P, 4), np.float32)
    for l in range(DEPTH):
        clay[l, :, 0:3] = (lam_init[l], 1 - lam_init[l], l * NEXP)
    freqs = (np.float32(10000.0) ** (-np.arange(16, dtype=np.float32) / np.float32(16))).astype(np.float32)
    tok = np.arange(LAT)
    rope = np.zeros((P, NL, 2, 64), np.float32)
    for axis, pos in enumerate((tok // GRID_W, tok % GRID_W)):
        ang = pos.astype(np.float32)[:, None] * freqs
        for half in range(2):
            o = axis * 32 + half * 16
            rope[:, :, 0, o:o + 16] = np.cos(ang).reshape(NL, P, 16).transpose(1, 0, 2)
            rope[:, :, 1, o:o + 16] = (np.sin(ang) * (1 if half else -1)).reshape(NL, P, 16).transpose(1, 0, 2)
    edge = np.zeros((P, 4, 16), np.float32)
    for g, win in enumerate(POOL_WINDOWS):
        for i in range(8):
            edge[:, g, i] = 1.0 / (i + win - win // 2 - max(i - win // 2, 0))
            j = SEQ - 8 + i
            edge[:, g, 8 + i] = 1.0 / (min(j + win - win // 2, SEQ) - (j - win // 2))
    qcol = (np.arange(NJ)[:, None] * QB + np.arange(QB))
    kcol = np.array(COL0)[:, None] + np.arange(KB)
    wstart = np.clip(qcol - WIN_C // 2, 0, GRID_W - WIN_C)
    rel = kcol[:, None, :] - wstart[:, :, None]
    valid = (rel >= 0) & (rel < WIN_C)
    m = np.where(valid, 0.0, NEG_INF).astype(np.float32).transpose(1, 0, 2)
    mask = np.tile(m, (ROWS, 1, 1))
    drow = np.arange(ROWS)[None, :] - np.arange(ROWS)[:, None] + WIN_R - 1
    dcol = np.clip(kcol[:, None, :] - qcol[:, :, None] + WIN_C - 1, 0, 2 * WIN_C - 2)
    rb = a["nat_rel_bias"][:, :, drow[:, None, None, :, None], dcol.transpose(1, 0, 2)[None, :, :, None, :]]
    bias = rb.reshape(DEPTH * 8, P, NJ, ROWS * KB)

    x = np.concatenate([a["x_sample"][0], a["x_prompt"][0]])
    arrays = {
        "xT": x.reshape(NT, P, KD, P).transpose(3, 0, 2, 1),
        "cT": np.stack([_chans(a["c"][0]), _chans(a["c_ctx"])], axis=2),
        "w": np.concatenate(stream), "small": np.stack(small), "rowg": np.concatenate(rowg), "lamrow": np.concatenate(lamrow),
        "clay": clay, "poolw": a["pool_w"].transpose(0, 2, 1, 3),
        "subk": a["peer_sub_keys"].reshape(DEPTH, 16, NKEYS, P).transpose(0, 3, 1, 2),
        "rope": rope, "edge": edge, "mask": mask, "bias": bias,
        "ckn": a["cache_nat_k"][0].reshape(DEPTH, PAST, 4, P).transpose(0, 3, 2, 1),
        "ckd": a["cache_diff_k"][0].reshape(DEPTH, PAST, 4, P).transpose(0, 3, 2, 1),
        "cvn": a["cache_nat_v"][0].reshape(DEPTH, PAST, BW), "cvd": a["cache_diff_v"][0].reshape(DEPTH, PAST, BW),
        "experts": np.concatenate([a["peer_u"].reshape(-1, D), a["peer_v"].reshape(-1, D)], axis=1),
    }
    arrays = {k: np.ascontiguousarray(v) for k, v in arrays.items()}
    outs = {"y_prompt": (SEQ, D), "y_sample": (LAT, D), "o_nk": (DEPTH * SEQ, BW), "o_nv": (DEPTH * SEQ, BW),
            "o_dk": (DEPTH * SEQ, BW), "o_dv": (DEPTH * SEQ, BW)}
    nc = bacc.Bacc("TRN2", target_bir_lowering=False, num_devices=1)
    args = {k: nc.dram_tensor(k, v.shape, F32, kind="ExternalInput").ap() for k, v in arrays.items()}
    args |= {k: nc.dram_tensor(k, s, F32, kind="ExternalOutput").ap() for k, s in outs.items()}
    backbone(nc, **args)
    r = run_bass_kernel_spmd(nc, [arrays], core_ids=[0]).results[0]
    return (r["y_prompt"].reshape(1, SEQ, D), r["y_sample"].reshape(1, LAT, D),
            r["o_nk"].reshape(1, DEPTH, SEQ, 8, 64), r["o_nv"].reshape(1, DEPTH, SEQ, 8, 64),
            r["o_dk"].reshape(1, DEPTH, SEQ, 4, 2, 64), r["o_dv"].reshape(1, DEPTH, SEQ, 4, 128))
```
